# Optimizing a Trainium2 kernel written in Bass

```python
import math
import jax, jax.numpy as jnp
from jax import lax
import numpy as np

D_MODEL = 1024
BATCH = 1
SEQ = 256
DEPTH = 2

N_EVEN = (DEPTH + 1) // 2
N_ODD = DEPTH // 2
HEAD_DIM = 64
ATT_HEADS = 8
ATT_WIDTH = ATT_HEADS * HEAD_DIM
DILATED_BRANCHES = ((128, 1), (512, 4), (2048, 16))
ATT_QBLOCK = 64
ROPE_THETA = 10000.0
SGU_GROUPS = 8
SGU_DIM = 64
SGU_WIDTH = SGU_GROUPS * SGU_DIM
SGU_CHUNK = 128
IN_WIDTH = 3 * ATT_WIDTH + 2 * SGU_WIDTH
MIX_WIDTH = ATT_WIDTH + SGU_WIDTH
S5_GROUP = 16
S5_GROUPS = D_MODEL // S5_GROUP
S5_STATE = 64
PEER_HEADS = 8
PEER_QDIM = 256
PEER_HALF = PEER_QDIM // 2
PEER_NKEYS = 128
PEER_EXPERTS = PEER_NKEYS * PEER_NKEYS
PEER_TOPK = 16
PEER_TBLOCK = 128
RMS_EPS = 1e-6
LN_EPS = 1e-5

kernel_name = 'hybrid_dilated_sgu_s5_peer'

def rmsnorm(x, g):
    xf = x.astype(jnp.float32)
    y = xf * lax.rsqrt(jnp.mean(xf * xf, axis=-1, keepdims=True) + RMS_EPS)
    return (y * g.astype(jnp.float32)).astype(x.dtype)

def rotary(x, pos):
    half = HEAD_DIM // 2
    inv = jnp.power(ROPE_THETA, -2.0 * jnp.arange(half, dtype=jnp.float32) / HEAD_DIM)
    ang = pos[:, None] * inv[None, :]
    cos = jnp.cos(ang)[None, :, None, :]
    sin = jnp.sin(ang)[None, :, None, :]
    xf = x.astype(jnp.float32)
    x1, x2 = xf[..., :half], xf[..., half:]
    return jnp.concatenate([x1 * cos - x2 * sin, x2 * cos + x1 * sin], axis=-1).astype(x.dtype)

def dilated_attention(q, k, v):
    b, h, s, hd = q.shape
    n_blk = s // ATT_QBLOCK
    scale = HEAD_DIM ** -0.5

    def block(i):
        start = i * ATT_QBLOCK
        qb = lax.dynamic_slice_in_dim(q, start, ATT_QBLOCK, axis=2)
        t = start + jnp.arange(ATT_QBLOCK)
        outs, lses = [], []
        for window, dil in DILATED_BRANCHES:
            steps = jnp.arange(window // dil + 1)
            pos = t[:, None] - dil * steps[None, :]
            valid = pos >= 0
            pos = jnp.maximum(pos, 0)
            kg = k[:, :, pos]
            vg = v[:, :, pos]
            sc = jnp.einsum('bhqd,bhqld->bhql', qb, kg, preferred_element_type=jnp.float32) * scale
            sc = jnp.where(valid, sc, -jnp.inf)
            m = jnp.max(sc, axis=-1)
            p = jnp.exp(sc - m[..., None])
            den = jnp.sum(p, axis=-1)
            outs.append(jnp.einsum('bhql,bhqld->bhqd', p, vg.astype(jnp.float32)) / den[..., None])
            lses.append(m + jnp.log(den))
        w = jax.nn.softmax(jnp.stack(lses), axis=0)
        return jnp.einsum('rbhq,rbhqd->bhqd', w, jnp.stack(outs))

    out = lax.map(block, jnp.arange(n_blk))
    return out.transpose(1, 0, 3, 2, 4).reshape(b, s, h * hd)

def hybrid_ab(h, w_in, sgu_norm_g, sgu_w, sgu_b, w_out):
    b, s, _ = h.shape
    z = h @ w_in
    q, k, v, zb = jnp.split(z, [ATT_WIDTH, 2 * ATT_WIDTH, 3 * ATT_WIDTH], axis=-1)
    pos = jnp.arange(s, dtype=jnp.float32)
    q = rotary(q.reshape(b, s, ATT_HEADS, HEAD_DIM), pos).transpose(0, 2, 1, 3)
    k = rotary(k.reshape(b, s, ATT_HEADS, HEAD_DIM), pos).transpose(0, 2, 1, 3)
    v = v.reshape(b, s, ATT_HEADS, HEAD_DIM).transpose(0, 2, 1, 3)
    att = dilated_attention(q, k, v).astype(h.dtype)
    zb = jax.nn.gelu(zb)
    u, g = jnp.split(zb, 2, axis=-1)
    gf = g.reshape(b, s, SGU_GROUPS, SGU_DIM).astype(jnp.float32)
    mu = jnp.mean(gf, axis=-1, keepdims=True)
    var = jnp.mean(jnp.square(gf - mu), axis=-1, keepdims=True)
    gf = (gf - mu) * lax.rsqrt(var + LN_EPS) * sgu_norm_g.astype(jnp.float32)
    gc = gf.reshape(b, s // SGU_CHUNK, SGU_CHUNK, SGU_GROUPS, SGU_DIM)
    w_causal = jnp.tril(sgu_w.astype(jnp.float32))
    sp = jnp.einsum('hij,bcjhd->bcihd', w_causal, gc) + sgu_b.astype(jnp.float32).T[:, :, None]
    sgu = (u.astype(jnp.float32) * sp.reshape(b, s, SGU_WIDTH)).astype(h.dtype)
    return jnp.concatenate([att, sgu], axis=-1) @ w_out

def s5_block(h, lam_re, lam_im, b_re, b_im, c_re, c_im, d_skip, log_step, glu_w, glu_b):
    b, s, _ = h.shape
    hf = h.astype(jnp.float32)
    u = hf.reshape(b, s, S5_GROUPS, S5_GROUP)
    dt = jnp.exp(log_step.astype(jnp.float32))[:, None]
    lr = lam_re.astype(jnp.float32)
    li = lam_im.astype(jnp.float32)
    decay = jnp.exp(lr * dt)
    ar = decay * jnp.cos(li * dt)
    ai = decay * jnp.sin(li * dt)
    mag = lr * lr + li * li
    kr = ((ar - 1.0) * lr + ai * li) / mag
    ki = (ai * lr - (ar - 1.0) * li) / mag
    br = b_re.astype(jnp.float32)
    bi = b_im.astype(jnp.float32)
    bbr = kr[..., None] * br - ki[..., None] * bi
    bbi = kr[..., None] * bi + ki[..., None] * br
    xr = jnp.einsum('bsgc,gpc->bsgp', u, bbr)
    xi = jnp.einsum('bsgc,gpc->bsgp', u, bbi)
    a_r = jnp.broadcast_to(ar, (1, s) + ar.shape)
    a_i = jnp.broadcast_to(ai, (1, s) + ai.shape)

    def combine(e1, e2):
        a1r, a1i, b1r, b1i = e1
        a2r, a2i, b2r, b2i = e2
        return (a2r * a1r - a2i * a1i, a2r * a1i + a2i * a1r,
                a2r * b1r - a2i * b1i + b2r, a2r * b1i + a2i * b1r + b2i)

    _, _, sr, si = lax.associative_scan(combine, (a_r, a_i, xr, xi), axis=1)
    y = (jnp.einsum('bsgp,gcp->bsgc', sr, c_re.astype(jnp.float32))
         - jnp.einsum('bsgp,gcp->bsgc', si, c_im.astype(jnp.float32)))
    y = y.reshape(b, s, D_MODEL) + d_skip.astype(jnp.float32) * hf
    g = jax.nn.gelu(y)
    out = g * jax.nn.sigmoid(g @ glu_w.astype(jnp.float32) + glu_b.astype(jnp.float32))
    return out.astype(h.dtype)

def peer(h, wq, subkeys, u_tab, v_tab):
    b, s, d = h.shape
    xt = h.reshape(-1, d)
    t = xt.shape[0]
    q = (xt @ wq).reshape(t, PEER_HEADS, 2, PEER_HALF)
    sc = jnp.einsum('thpc,pkc->thpk', q, subkeys, preferred_element_type=jnp.float32)
    sv, si = lax.top_k(sc, PEER_TOPK)
    cand = sv[:, :, 0, :, None] + sv[:, :, 1, None, :]
    cidx = si[:, :, 0, :, None] * PEER_NKEYS + si[:, :, 1, None, :]
    cs, cpos = lax.top_k(cand.reshape(t, PEER_HEADS, -1), PEER_TOPK)
    idx = jnp.take_along_axis(cidx.reshape(t, PEER_HEADS, -1), cpos, axis=-1)
    gate = jax.nn.softmax(cs, axis=-1)
    nb = t // PEER_TBLOCK
    idx = idx.reshape(nb, PEER_TBLOCK, PEER_HEADS * PEER_TOPK)
    gate = gate.reshape(nb, PEER_TBLOCK, PEER_HEADS * PEER_TOPK)
    xb = xt.reshape(nb, PEER_TBLOCK, d)

    def expert_block(args):
        xbb, ib, gb = args
        act = jax.nn.gelu(jnp.einsum('td,tkd->tk', xbb, u_tab[ib], preferred_element_type=jnp.float32))
        return jnp.einsum('tk,tkd->td', gb * act, v_tab[ib].astype(jnp.float32))

    y = lax.map(expert_block, (xb, idx, gate))
    return y.reshape(b, s, d).astype(h.dtype)

def setup_inputs(seed: int = 0) -> dict:
    key = jax.random.key(seed)
    ks = iter(jax.random.split(key, 32))

    def nrm(shape, scale):
        return scale * jax.random.normal(next(ks), shape, jnp.float32)

    n = jnp.arange(S5_STATE, dtype=jnp.float32)
    return {
        'x': nrm((BATCH, SEQ, D_MODEL), 1.0),
        'norm_mix_g': 1.0 + nrm((DEPTH, D_MODEL), 0.02),
        'norm_ffn_g': 1.0 + nrm((DEPTH, D_MODEL), 0.02),
        'final_norm_g': 1.0 + nrm((D_MODEL,), 0.02),
        'mix_w_in': nrm((N_EVEN, D_MODEL, IN_WIDTH), D_MODEL ** -0.5),
        'sgu_norm_g': 1.0 + nrm((N_EVEN, SGU_GROUPS, SGU_DIM), 0.02),
        'sgu_w': nrm((N_EVEN, SGU_GROUPS, SGU_CHUNK, SGU_CHUNK), SGU_CHUNK ** -0.5),
        'sgu_b': 1.0 + nrm((N_EVEN, SGU_GROUPS, SGU_CHUNK), 0.02),
        'mix_w_out': nrm((N_EVEN, MIX_WIDTH, D_MODEL), MIX_WIDTH ** -0.5),
        's5_lambda_re': -0.5 + nrm((N_ODD, S5_GROUPS, S5_STATE), 0.01),
        's5_lambda_im': math.pi * n + nrm((N_ODD, S5_GROUPS, S5_STATE), 0.01),
        's5_b_re': nrm((N_ODD, S5_GROUPS, S5_STATE, S5_GROUP), (2 * S5_GROUP) ** -0.5),
        's5_b_im': nrm((N_ODD, S5_GROUPS, S5_STATE, S5_GROUP), (2 * S5_GROUP) ** -0.5),
        's5_c_re': nrm((N_ODD, S5_GROUPS, S5_GROUP, S5_STATE), S5_STATE ** -0.5),
        's5_c_im': nrm((N_ODD, S5_GROUPS, S5_GROUP, S5_STATE), S5_STATE ** -0.5),
        's5_d': nrm((N_ODD, D_MODEL), 1.0),
        's5_log_step': jax.random.uniform(next(ks), (N_ODD, S5_GROUPS), jnp.float32,
                                          minval=math.log(1e-3), maxval=math.log(1e-1)),
        'glu_w': nrm((N_ODD, D_MODEL, D_MODEL), D_MODEL ** -0.5),
        'glu_b': nrm((N_ODD, D_MODEL), 0.01),
        'peer_wq': nrm((DEPTH, D_MODEL, PEER_HEADS * PEER_QDIM), D_MODEL ** -0.5),
        'peer_subkeys': nrm((DEPTH, 2, PEER_NKEYS, PEER_HALF), PEER_HALF ** -0.5),
        'peer_u': nrm((DEPTH, PEER_EXPERTS, D_MODEL), D_MODEL ** -0.5),
        'peer_v': nrm((DEPTH, PEER_EXPERTS, D_MODEL), PEER_HEADS ** -0.5),
    }

def reference(x, norm_mix_g, norm_ffn_g, final_norm_g, mix_w_in, sgu_norm_g, sgu_w, sgu_b,
              mix_w_out, s5_lambda_re, s5_lambda_im, s5_b_re, s5_b_im, s5_c_re, s5_c_im,
              s5_d, s5_log_step, glu_w, glu_b, peer_wq, peer_subkeys, peer_u, peer_v):
    for layer in range(DEPTH):
        j = layer // 2
        h = rmsnorm(x, norm_mix_g[layer])
        if layer % 2 == 0:
            x = x + hybrid_ab(h, mix_w_in[j], sgu_norm_g[j], sgu_w[j], sgu_b[j], mix_w_out[j])
        else:
            x = x + s5_block(h, s5_lambda_re[j], s5_lambda_im[j], s5_b_re[j], s5_b_im[j],
                             s5_c_re[j], s5_c_im[j], s5_d[j], s5_log_step[j], glu_w[j], glu_b[j])
        h = rmsnorm(x, norm_ffn_g[layer])
        x = x + peer(h, peer_wq[layer], peer_subkeys[layer], peer_u[layer], peer_v[layer])
    return rmsnorm(x, final_norm_g)


_drawn_inputs = setup_inputs


def setup_inputs(seed=0):
    import zlib

    import numpy as np

    out = dict(_drawn_inputs(seed))
    spreads = {}
    factors = {'final_norm_g': 27.582,
     'sgu_norm_g': 8.797,
     's5_lambda_re': 200.0,
     'glu_b': 32.29,
     'sgu_b': 2.926,
     's5_lambda_im': 31.84,
     's5_b_re': 38.728,
     's5_b_im': 38.32,
     's5_c_re': 41.056,
     's5_c_im': 39.984,
     's5_log_step': 36.016,
     'norm_ffn_g': 2.69}
    for name, (base, spread) in spreads.items():
        noise = np.random.default_rng([zlib.crc32(name.encode()), seed]).standard_normal(out[name].shape)
        drawn = base * np.exp(spread * noise) if base else spread * noise
        out[name] = __import__('jax').numpy.asarray(drawn.astype(out[name].dtype))
    for name, factor in factors.items():
        out[name] = (out[name] * factor).astype(out[name].dtype)
    return out
```

```python
import math
from contextlib import ExitStack

import concourse.bass as bass
from concourse import mybir

ALU = mybir.AluOpType
ACT = mybir.ActivationFunctionType
AX = mybir.AxisListType
F32 = mybir.dt.float32
U32 = mybir.dt.uint32

P = 128
SEQ = 256
D = 1024
T = SEQ // P
KC = D // P
HEADS, HD = 8, 64
AW = HEADS * HD
WIN = 3 * AW + 2 * 512
BANK = 512
PH, NK, TOPK = 8, 128, 16
QW = PH * 2 * P
EXPERTS = NK * NK
GROUPS = T * PH
UR, VR = 8, 16
S5_TILES = 32
RMS_EPS, LN_EPS = 1e-6, 1e-5
SCALE = HD ** -0.5
LOWEST = -3.0e38
ROUND = 12582912.0
TWO_PI_HI = 6.28125
TWO_PI_LO = 2 * math.pi - 6.28125
INV_TWO_PI = 1 / (2 * math.pi)
TURN = 6.2831845
PI_BELOW = 3.1415925

C_ID, C_CNT, C_NEG, C_COS, C_SIN, C_NSIN, C_IOTA, C_TIME, C_HPI = 0, 128, 512, 896, 960, 1024, 1088, 1104, 1360
C_ALL = 1361


def trunk(nc, x_in, gains, cst_in, w_in, sgu_g, sgu_wT, sgu_bT, w_out, s5_par, s5_b, s5_c, s5_dv, glu_bv, glu_w,
          wq, skT, u_tab, v_tab, out):
    with ExitStack() as ctx:
        def sb(name, shape, dt=F32):
            return ctx.enter_context(nc.sbuf_tensor(name, shape, dt))

        def sem(name):
            return ctx.enter_context(nc.semaphore(name))

        x = sb("x", [P, T, D])
        h = sb("h", [P, T, D])
        hT = sb("hT", [P, KC, SEQ])
        cst = sb("cst", [P, C_ALL])
        gain = sb("gain", [P, D])
        zeros = sb("zeros", [P, P])
        sk = sb("sk", [P, 2, 2, NK])
        ss, ms, sd, rstd = (sb(n, [P, T]) for n in ("ss", "ms", "sd", "rstd"))
        big = sb("big", [P, (UR + VR) * D])
        w2 = sb("w2", [P, KC * D])
        tmp = sb("tmp", [P, 8192])
        sgw = sb("sgw", [P, D])
        ps = [ctx.enter_context(nc.psum_tensor(f"ps{i}", [P, BANK], F32)) for i in range(8)]

        ident = cst[:, C_ID:C_ID + P]
        count = [cst[:, C_CNT + P * t:C_CNT + P * (2 * t + 1)] for t in range(T)]
        negm = [cst[:, C_NEG + P * t:C_NEG + P * (2 * t + 1)] for t in range(T)]
        cos_t = cst[:, C_COS:C_COS + 64].rearrange("p (t k) -> p t k", t=T)
        sin_t = cst[:, C_SIN:C_SIN + 64].rearrange("p (t k) -> p t k", t=T)
        nsin_t = cst[:, C_NSIN:C_NSIN + 64].rearrange("p (t k) -> p t k", t=T)
        iota16 = cst[:, C_IOTA:C_IOTA + 16]
        time_row = cst[:, C_TIME:C_TIME + SEQ]
        half_pi = cst[:, C_HPI:C_HPI + 1]

        win = big[:, 0:KC * WIN].rearrange("p (k n) -> p k n", k=KC)
        wout = w2[:, :].rearrange("p (k n) -> p k n", k=KC)
        qk = tmp[:, 0:2048].rearrange("p (t n) -> p t n", t=T)
        rot_a, rot_b = tmp[:, 2048:2560], tmp[:, 2560:3072]
        vv = tmp[:, 3072:4096].rearrange("p (t n) -> p t n", t=T)
        zu = tmp[:, 4096:5120].rearrange("p (t n) -> p t n", t=T)
        zg = tmp[:, 5120:6144].rearrange("p (t n) -> p t n", t=T)
        sg_tmp = tmp[:, 6144:6656]
        sg_gain = tmp[:, 6656:7168]
        aqT = big[:, 0:1024].rearrange("p (a s) -> p a s", a=4)
        akT = big[:, 1024:2048].rearrange("p (a s) -> p a s", a=4)
        E = [big[:, 2048 + BANK * u:2560 + BANK * u] for u in range(6)]
        PT = [big[:, 5120 + BANK * u:5632 + BANK * u] for u in range(6)]
        negmax, den, rden = (sb(n, [P, 16]) for n in ("negmax", "den", "rden"))
        mu, var, lsd, lrs = (sb(n, [P, 8]) for n in ("mu", "var", "lsd", "lrs"))
        sgb = sb("sgb", [P, 8])

        wqs = big[:, UR * D:].rearrange("p (k n) -> p k n", k=KC)
        ringu = big[:, 0:UR * D].rearrange("p (b n) -> p b n", b=UR)
        ringv = big[:, UR * D:].rearrange("p (b n) -> p b n", b=VR)
        qT = w2[:, 0:16 * SEQ].rearrange("p (a s) -> p a s", a=16)
        S = tmp[:, 0:4096].rearrange("p (g k) -> p g k", g=GROUPS)
        diag = [tmp[:, 4096 + 2048 * i:6144 + 2048 * i].rearrange("p (s t) -> p s t", s=TOPK) for i in range(2)]
        key_a, key_b = sb("key_a", [P, 2, NK]), sb("key_b", [P, 2, NK])
        cand_a, cand_b = (k[:, :, :].rearrange("p a k -> p (a k)") for k in (key_a, key_b))
        top = sb("top", [P, 2, TOPK])
        top_i = sb("top_i", [P, 2, TOPK], U32)
        top_f = sb("top_f", [P, 2, TOPK])
        pos_i = sb("pos_i", [P, TOPK], U32)
        pos_ab = sb("pos_ab", [P, 2, TOPK], U32)
        row = sb("row", [P, 2, TOPK])
        idx_all = sb("idx_all", [P, GROUPS, TOPK], U32)
        idx = [sb(f"idx{i}", [P, TOPK], U32) for i in range(2)]
        cs = [sb(f"cs{i}", [P, TOPK]) for i in range(2)]
        ncs = [sb(f"ncs{i}", [P, 1]) for i in range(2)]
        gexp = [sb(f"gexp{i}", [P, TOPK]) for i in range(2)]
        gsum = [sb(f"gsum{i}", [P, 1]) for i in range(2)]
        grec = [sb(f"grec{i}", [P, 1]) for i in range(2)]
        dots = [sb(f"dots{i}", [P, TOPK]) for i in range(2)]
        gel = [sb(f"gel{i}", [P, TOPK]) for i in range(2)]
        wgt = [sb(f"wgt{i}", [P, TOPK]) for i in range(2)]

        s5p = sb("s5p", [P, 3 * S5_TILES])
        lam_r, lam_i, log_step = (s5p[:, S5_TILES * i:S5_TILES * (i + 1)] for i in range(3))
        s5s = sb("s5s", [P, 14, S5_TILES])
        (dt_, lrdt, th, dec, kf, ab, sn_, cs_, ar, ai, mag, kr, ki, thp) = (s5s[:, i, :] for i in range(14))
        dskip, glub = sb("dskip", [P, KC]), sb("glub", [P, KC])
        b_raw = tmp[:, 0:1024].rearrange("p (r n) -> p r n", r=2)
        bt1, bt2 = tmp[:, 1024:1536], tmp[:, 1536:2048]
        prod = [tmp[:, 512 * i:512 * (i + 1)].rearrange("p (r s) -> p r s", r=2) for i in range(2)]
        zst = [tmp[:, 1024 + 512 * i:1536 + 512 * i].rearrange("p (r s) -> p r s", r=2) for i in range(2)]
        dem = [[tmp[:, 2048 + 1024 * i + 512 * j:2560 + 1024 * i + 512 * j].rearrange("p (r s) -> p r s", r=2)
                for j in range(2)] for i in range(2)]
        cz = tmp[:, 4096:5760]
        bT = tmp[:, 5760:7808].rearrange("p (b n) -> p b n", b=16)
        sig = tmp[:, 0:2048].rearrange("p (k s) -> p k s", k=KC)
        oT = tmp[:, 2048:4096].rearrange("p (k s) -> p k s", k=KC)
        tab = [big[:, 2048 * i:2048 * (i + 1)].rearrange("p (r j s) -> p r j s", r=2, j=4) for i in range(2)]
        ph = big[:, 4096:5120].rearrange("p (j s) -> p j s", j=4)
        pk = big[:, 5120:6144].rearrange("p (j s) -> p j s", j=4)
        bs = big[:, 6144:8192].rearrange("p (c r j g n) -> p c r j g n", c=8, r=2, j=4, g=2)
        c_raw = sgw[:, :].rearrange("p (r i n) -> p r i n", r=2, i=S5_TILES)
        gT = h[:, :, :].rearrange("p t (a s) -> p (t a) s", a=4)
        gluw = w2[:, :].rearrange("p (k n) -> p k n", k=KC)

        ld_x = [sem(f"ld_x{t}") for t in range(T)]
        ld_gain, ld_cst, ld_sgu, ld_wout, ld_sk, ld_s5, ld_glu, ld_c, ld_b = (
            sem(n) for n in ("ld_gain", "ld_cst", "ld_sgu", "ld_wout", "ld_sk", "ld_s5", "ld_glu", "ld_c", "ld_b"))
        ld_win = [sem(f"ld_win{n}") for n in range(5)]
        ld_wq = [sem(f"ld_wq{n}") for n in range(4)]
        ld_out = [sem(f"ld_out{t}") for t in range(T)]
        got_u = [sem(f"got_u{b}") for b in range(UR)]
        got_v = [sem(f"got_v{b}") for b in range(VR)]
        sq_done, ms_done, sd_done, h_done, nT_done, hT_act, hT_dve, x_done = (
            sem(n) for n in ("sq_done", "ms_done", "sd_done", "h_done", "nT_done", "hT_act", "hT_dve", "x_done"))
        (z_done, z_dve, z_act, sgm_ok, qkT_done, qT_act, kT_dve, lnv_done, lsd_done, g_done, sc_done, nm_done, ex_done,
         p_done, pT_done, pT_act, sp_done, o_done, mix_done, mT_done, mT_act, mT_dve, wo_done) = (sem(n) for n in (
             "z_done", "z_dve", "z_act", "sgm_ok", "qkT_done", "qT_act", "kT_dve", "lnv_done", "lsd_done", "g_done",
             "sc_done", "nm_done", "ex_done", "p_done", "pT_done", "pT_act", "sp_done", "o_done", "mix_done",
             "mT_done", "mT_act", "mT_dve", "wo_done"))
        (q_done, q_act, q_dve, s_done, s_act, idx_ok, cs_ok, exp_ok, u_free, v_free, gel_ok, diag_ok,
         y_done, zero_ok) = (sem(n) for n in (
             "q_done", "q_act", "q_dve", "s_done", "s_act", "idx_ok", "cs_ok", "exp_ok", "u_free", "v_free",
             "gel_ok", "diag_ok", "y_done", "zero_ok"))
        (dt_ok, th_ok, dec_ok, thr_ok, cs5_ok, b_ok, bT_done, bT_act, ph_ok, tab_ok, xs_done, w_ok, st_ok, d_ok,
         cz_zero, cz_ok, yc_done, ye_ok, g_ok, gl_done, sig_ok, o_ok, back_done, tz_ok) = (sem(n) for n in (
             "dt_ok", "th_ok", "dec_ok", "thr_ok", "cs5_ok", "b_ok", "bT_done", "bT_act", "ph_ok", "tab_ok", "xs_done",
             "w_ok", "st_ok", "d_ok", "cz_zero", "cz_ok", "yc_done", "ye_ok", "g_ok", "gl_done", "sig_ok", "o_ok",
             "back_done", "tz_ok"))

        block = ctx.enter_context(nc.Block())
        COLS = [0, 1, 2, 4, 3]
        ABANK = [4, 5, 6, 7, 0, 1]
        TBANK = [4, 5, 6, 7, 4, 5]

        def unit(u):
            return (0, u, 4, P) if u < 2 else (1, u % 2 + 4 * (u // 4), 2, 2 * P)

        def bc(ap, dims):
            at = dims.index(None)
            for _ in range(at):
                ap = ap.unsqueeze(1)
            for _ in range(len(dims) - 1 - at):
                ap = ap.unsqueeze(len(ap.shape))
            return ap.to_broadcast([ap.shape[0]] + [ap.shape[1 + at] if d is None else d for d in dims])

        @block.sync
        def _(sp):
            for t in range(T):
                sp.dma_start(x[:, t, :], x_in[t * P:(t + 1) * P, :]).then_inc(ld_x[t], 16)
            sp.dma_start(gain[:, :], gains[0:1, :].to_broadcast([P, D])).then_inc(ld_gain, 16)
            sp.dma_start(cst[:, :], cst_in).then_inc(ld_cst, 16)
            w_v = w_in.rearrange("(k p) n -> p k n", p=P)
            for i, n in enumerate(COLS):
                sp.dma_start(win[:, :, n * BANK:(n + 1) * BANK], w_v[:, :, n * BANK:(n + 1) * BANK]).then_inc(ld_win[i], 16)
            sp.dma_start(s5p[:, :], s5_par).then_inc(ld_s5, 16)
            sp.dma_start(dskip[:, :], s5_dv).then_inc(ld_s5, 16)
            sp.dma_start(glub[:, :], glu_bv).then_inc(ld_s5, 16)
            sp.dma_start(sgw[:, :], sgu_wT).then_inc(ld_sgu, 16)
            sp.dma_start(sg_gain, sgu_g.to_broadcast([P, AW])).then_inc(ld_sgu, 16)
            sp.dma_start(sgb[:, :], sgu_bT).then_inc(ld_sgu, 16)
            sp.dma_start(wout, w_out.rearrange("(k p) n -> p k n", p=P)).then_inc(ld_wout, 16)
            sp.dma_start(sk[:, :, :, :], skT).then_inc(ld_sk, 16)

            def load_gain(k):
                sp.wait_ge(h_done, 2 * k)
                sp.dma_start(gain[:, :], gains[k:k + 1, :].to_broadcast([P, D])).then_inc(ld_gain, 16)

            def load_wq(layer):
                q_v = wq[layer].rearrange("(k p) n -> p k n", p=P)
                for n in range(4):
                    sp.dma_start(wqs[:, :, n * BANK:(n + 1) * BANK],
                                 q_v[:, :, n * BANK:(n + 1) * BANK]).then_inc(ld_wq[n], 16)

            load_gain(1)
            sp.wait_ge(z_done, 2 * len(COLS))
            load_wq(0)
            load_gain(2)
            sp.wait_ge(sp_done, T)
            sp.dma_start(c_raw, s5_c).then_inc(ld_c, 16)
            sp.wait_ge(s_done, 8)
            sp.dma_start(gluw, glu_w.rearrange("(k p) n -> p k n", p=P)).then_inc(ld_glu, 16)
            sp.wait_ge(y_done, T)
            sp.dma_start(b_raw, s5_b).then_inc(ld_b, 16)
            load_wq(1)
            load_gain(3)
            load_gain(4)
            for t in range(T):
                sp.wait_ge(h_done, 8 + t + 1)
                sp.dma_start(out[t * P:(t + 1) * P, :], h[:, t, :]).then_inc(ld_out[t], 16)
            for t in range(T):
                sp.wait_ge(ld_out[t], 16)

        @block.gpsimd
        def _(pool):
            pool.wait_ge(ld_sgu, 48)
            nc.gpsimd.affine_select(out=sgw[:, :].rearrange("p (h i) -> p h i", h=8),
                                    in_=sgw[:, :].rearrange("p (h i) -> p h i", h=8),
                                    pattern=[[0, 8], [1, P]], compare_op=ALU.is_ge, fill=0.0, base=0,
                                    channel_multiplier=-1).then_inc(sgm_ok, 1)

            def gather_group(layer, n, par):
                N = n + GROUPS * layer
                pool.wait_ge(idx_ok, N + 1)
                pool.wait_ge(v_free, N * 16 + 16)
                pool.nop(nofuse=True)
                nc.gpsimd.tensor_copy(idx[par][:, :], idx_all[:, bass.ds(n, 1), :].rearrange("p a k -> p (a k)"))
                pool.drain()
                for s in range(TOPK):
                    if s % 4 == 0:
                        pool.wait_ge(u_free, N * 16 + (s + 4))
                        pool.nop(nofuse=True)
                    nc.gpsimd.indirect_dma_start(
                        out=ringu[:, s % UR, :], out_offset=None, in_=u_tab,
                        in_offset=bass.IndirectOffsetOnAxis(ap=idx[par][:, s:s + 1], axis=0)).then_inc(got_u[s % UR], 16)
                for s in range(TOPK):
                    if s % 4 == 0:
                        pool.wait_ge(v_free, N * 16 + (s + 4 + 16))
                        pool.nop(nofuse=True)
                    nc.gpsimd.indirect_dma_start(
                        out=ringv[:, s, :], out_offset=None, in_=v_tab,
                        in_offset=bass.IndirectOffsetOnAxis(ap=idx[par][:, s:s + 1], axis=0)).then_inc(got_v[s], 16)

            def gathers(layer):
                pool.wait_ge(q_done, 8 * (layer + 1))
                with pool.Fori(0, GROUPS // 2) as it:
                    gather_group(layer, it * 2, 0)
                    gather_group(layer, it * 2 + 1, 1)

            def s5_phases(c):
                if c > 0:
                    pool.wait_ge(tab_ok, c)
                nc.gpsimd.tensor_tensor(ph, bc(time_row, [4, None]), bc(thp[:, 4 * c:4 * c + 4], [None, SEQ]), ALU.mult)
                pool.drain()
                nc.gpsimd.tensor_scalar(pk, ph, ROUND, ROUND, ALU.add, ALU.subtract)
                pool.drain()
                nc.gpsimd.tensor_tensor(ph, ph, pk, ALU.subtract).then_inc(ph_ok, 1)
                pool.drain()

            gathers(0)
            pool.wait_ge(x_done, 8)
            nc.gpsimd.memset(cz, 0.0).then_inc(cz_zero, 1)
            s5_phases(0)
            for c in range(KC):
                if c + 1 < KC:
                    s5_phases(c + 1)
                for j in range(4):
                    i = 4 * c + j
                    pool.wait_ge(st_ok, 2 * (i + 1))
                    if i >= 2:
                        pool.wait_ge(yc_done, i - 1)
                    nc.gpsimd.tensor_tensor(dem[i % 2][0], zst[i % 2], bc(tab[c % 2][:, 0, j, :], [2, None]),
                                            ALU.mult).then_inc(d_ok, 1)
                    nc.gpsimd.tensor_tensor(dem[i % 2][1], zst[i % 2], bc(tab[c % 2][:, 1, j, :], [2, None]),
                                            ALU.mult).then_inc(d_ok, 1)
            gathers(1)

        @block.scalar
        def _(act):
            def norm(k):
                for t in range(T):
                    if k == 0:
                        act.wait_ge(ld_x[t], 16)
                    else:
                        act.wait_ge(x_done, 4 * (k - 1) + 2 * t + 2)
                    nc.scalar.activation(h[:, t, :], x[:, t, :], ACT.Square, accum_out=ss[:, t:t + 1]).then_inc(sq_done, 1)
                for t in range(T):
                    act.wait_ge(ms_done, 2 * k + t + 1)
                    nc.scalar.activation(sd[:, t:t + 1], ms[:, t:t + 1], ACT.Sqrt).then_inc(sd_done, 1)

            def norm_evac(k):
                for t in range(T):
                    act.wait_ge(nT_done, 4 * k + 2 * t + 1)
                    nc.scalar.activation(hT[:, 0:4, t * P:(t + 1) * P], ps[2 * t][:, :].rearrange("p (a s) -> p a s", a=4),
                                         ACT.Copy).then_inc(hT_act, 1)

            def peer(layer):
                for j in range(0, 8, 2):
                    act.wait_ge(q_done, 8 * layer + j + 1)
                    nc.scalar.activation(qT[:, 2 * j:2 * j + 2, :], ps[4 + j % 4][:, :].rearrange("p (a s) -> p a s", a=2),
                                         ACT.Copy).then_inc(q_act, 1)
                for i in range(8):
                    act.wait_ge(s_done, 8 * layer + i + 1)
                    nc.scalar.activation(S[:, 2 * i:2 * i + 2, :], ps[i % 4][:, :].rearrange("p (a s) -> p a s", a=2),
                                         ACT.Copy).then_inc(s_act, 1)

                def gate(n, par):
                    act.wait_ge(cs_ok, n + (GROUPS * layer + 1))
                    nc.scalar.activation(gexp[par][:, :], cs[par][:, :], ACT.Exp, bias=ncs[par][:, :],
                                         accum_out=gsum[par][:, :]).then_inc(exp_ok, 1)

                def gelu(n, par):
                    act.wait_ge(u_free, n * 16 + (16 * GROUPS * layer + 16 + UR))
                    nc.scalar.activation(gel[par][:, :], dots[par][:, :], ACT.Gelu_apprx_tanh).then_inc(gel_ok, 1)

                gate(0, 0)
                with act.Fori(0, GROUPS // 2 - 1) as it:
                    gate(it * 2 + 1, 1)
                    gelu(it * 2, 0)
                    gate(it * 2 + 2, 0)
                    gelu(it * 2 + 1, 1)
                gate(GROUPS - 1, 1)
                gelu(GROUPS - 2, 0)
                gelu(GROUPS - 1, 1)

            norm(0)
            norm_evac(0)
            act.wait_ge(ld_s5, 48)
            nc.scalar.activation(dt_, log_step, ACT.Exp).then_inc(dt_ok, 1)
            act.wait_ge(th_ok, 1)
            nc.scalar.activation(dec, lrdt, ACT.Exp).then_inc(dec_ok, 1)
            for m in range(4, 10):
                act.wait_ge(z_done, m + 1)
                dst, fn = ((vv, ACT.Copy), (zg, ACT.Gelu_apprx_tanh), (zu, ACT.Gelu_apprx_tanh))[m // 2 - 2]
                nc.scalar.activation(dst[:, m % 2, :], ps[4 + m % 4][:, :], fn).then_inc(z_act, 1)
            for t in range(T):
                act.wait_ge(qkT_done, t + 1)
                nc.scalar.activation(aqT[:, :, t * P:(t + 1) * P], ps[t][:, :].rearrange("p (a s) -> p a s", a=4),
                                     ACT.Copy).then_inc(qT_act, 1)
            for t in range(T):
                act.wait_ge(lnv_done, t + 1)
                nc.scalar.activation(lsd[:, :], var[:, :], ACT.Sqrt).then_inc(lsd_done, 1)
            for u in range(6):
                act.wait_ge(nm_done, u + 1)
                t, h0, nh, keys = unit(u)
                for i in range(nh):
                    c = 8 * t + h0 + 2 * i
                    ins = nc.scalar.activation(E[u][:, i * keys:(i + 1) * keys], E[u][:, i * keys:(i + 1) * keys],
                                               ACT.Exp, bias=negmax[:, c:c + 1])
                ins.then_inc(ex_done, 1)
            for u in range(6):
                act.wait_ge(pT_done, u + 1)
                nc.scalar.activation(PT[u], ps[TBANK[u]][:, :], ACT.Copy).then_inc(pT_act, 1)
            for t in range(T):
                act.wait_ge(mT_done, 2 * t + 1)
                nc.scalar.activation(hT[:, 0:4, t * P:(t + 1) * P], ps[2 + 4 * t][:, :].rearrange("p (a s) -> p a s", a=4),
                                     ACT.Copy).then_inc(mT_act, 1)
            act.wait_ge(thr_ok, 1)
            nc.scalar.activation(ab, th, ACT.Abs)
            nc.scalar.activation(sn_, th, ACT.Sin)
            act.drain()
            nc.scalar.activation(cs_, ab, ACT.Sin, bias=half_pi, scale=-1.0).then_inc(cs5_ok, 1)
            norm(1)
            norm_evac(1)
            peer(0)
            norm(2)
            norm_evac(2)
            for b in range(4):
                act.wait_ge(bT_done, b + 1)
                nc.scalar.activation(bT[:, 4 * b:4 * b + 4, :], ps[4 + b][:, :].rearrange("p (a s) -> p a s", a=4),
                                     ACT.Copy).then_inc(bT_act, 1)
            act.wait_ge(cz_zero, 1)
            act.wait_ge(ld_c, 16)

            def tables(c):
                act.wait_ge(ph_ok, c + 1)
                if c >= 2:
                    act.wait_ge(w_ok, 4 * (c - 1))
                    act.wait_ge(d_ok, 8 * (c - 1))
                nc.scalar.activation(tab[c % 2][:, 1, :, :], ph, ACT.Sin, scale=TURN)
                nc.scalar.activation(tab[c % 2][:, 0, :, :], ph, ACT.Abs)
                act.drain()
                nc.scalar.activation(tab[c % 2][:, 0, :, :], tab[c % 2][:, 0, :, :], ACT.Sin, bias=half_pi,
                                     scale=-TURN).then_inc(tab_ok, 1)

            tables(0)
            for c in range(KC):
                if c + 1 < KC:
                    tables(c + 1)
                if c > 0:
                    act.wait_ge(yc_done, 4 * c)
                for g in range(2):
                    half = slice(64 * g, 64 * g + 64)
                    dst = cz[half, :].rearrange("p (j y) -> p j y", j=4)
                    for v, (r, sign) in enumerate(((0, 1.0), (0, -1.0), (1, -1.0))):
                        nc.scalar.activation(dst[:, :, v * P + 16 * g:v * P + 16 * g + 16], c_raw[half, r, 4 * c:4 * c + 4, :],
                                             ACT.Copy, scale=sign).then_inc(cz_ok, 1)
            act.wait_ge(ye_ok, KC)
            nc.scalar.activation(gT, gT, ACT.Gelu_apprx_tanh).then_inc(g_ok, 1)
            for n in range(KC):
                act.wait_ge(gl_done, n + 1)
                nc.scalar.activation(sig[:, n, :], ps[6 + n % 2][:, 0:SEQ], ACT.Sigmoid,
                                     bias=glub[:, n:n + 1]).then_inc(sig_ok, 1)
            norm(3)
            norm_evac(3)
            peer(1)
            norm(4)

        @block.tensor
        def _(pe):
            def norm_transposes(k):
                for t in range(T):
                    pe.wait_ge(h_done, 2 * k + t + 1)
                    for b in range(2):
                        for a in range(4):
                            c = 4 * b + a
                            ins = nc.tensor.transpose(ps[2 * t + b][:, a * P:(a + 1) * P], h[:, t, c * P:(c + 1) * P], ident)
                        ins.then_inc(nT_done, 1)

            def wait_hT(k, t=T - 1):
                pe.wait_ge(hT_act, 2 * k + t + 1)
                pe.wait_ge(hT_dve, 2 * k + t + 1)

            def peer(layer):
                k_norm = 2 * layer + 1
                wait_hT(k_norm)
                for j in range(8):
                    pe.wait_ge(ld_wq[j // 2], 16 * (layer + 1))
                    if j >= 4:
                        if j % 2 == 0:
                            pe.wait_ge(q_act, 4 * layer + (j - 4) // 2 + 1)
                        else:
                            pe.wait_ge(q_dve, 4 * layer + (j - 4) // 2 + 1)
                    for a in range(2):
                        hp = 2 * j + a
                        for k in range(KC):
                            ins = nc.tensor.matmul(ps[4 + j % 4][:, a * SEQ:(a + 1) * SEQ], wqs[:, k, hp * P:(hp + 1) * P],
                                                   hT[:, k, :], start=(k == 0), stop=(k == KC - 1))
                    ins.then_inc(q_done, 1)
                pe.wait_ge(q_act, 4 * (layer + 1))
                pe.wait_ge(q_dve, 4 * (layer + 1))
                pe.wait_ge(ld_sk, 16)
                for i in range(8):
                    t = i // 4
                    if i >= 4:
                        pe.wait_ge(s_act, 8 * layer + i - 3)
                    for a in range(4):
                        hp = 4 * (i % 4) + a
                        ins = nc.tensor.matmul(ps[i % 4][:, a * P:(a + 1) * P], qT[:, hp, t * P:(t + 1) * P],
                                               sk[:, layer, hp % 2, :], start=True, stop=True)
                    ins.then_inc(s_done, 1)

                def experts(n, par, t):
                    N = n + GROUPS * layer
                    pe.wait_ge(diag_ok, N + 1)
                    for s in range(TOPK):
                        pe.wait_ge(got_v[s], N * 16 + 16)
                        for b in range(2):
                            ins = nc.tensor.matmul(ps[4 + 2 * t + b][:, :], diag[par][:, s, :],
                                                   ringv[:, s, b * BANK:(b + 1) * BANK], start=False, stop=False)
                        ins.then_inc(v_free, 1)

                pe.wait_ge(zero_ok, 1)
                for t in range(T):
                    for b in range(2):
                        nc.tensor.matmul(ps[4 + 2 * t + b][:, :], zeros[:, :], cst[:, C_CNT:C_CNT + BANK],
                                         start=True, stop=False)
                    with pe.Fori(0, PH // 2) as it:
                        experts(it * 2 + PH * t, 0, t)
                        experts(it * 2 + (PH * t + 1), 1, t)
                    for b in range(2):
                        ins = nc.tensor.matmul(ps[4 + 2 * t + b][:, :], zeros[:, :], cst[:, C_CNT:C_CNT + BANK],
                                               start=False, stop=True)
                    ins.then_inc(y_done, 1)

            pe.wait_ge(ld_cst, 16)
            norm_transposes(0)
            for m in range(10):
                ni, t = m // 2, m % 2
                n = COLS[ni]
                wait_hT(0, t)
                pe.wait_ge(ld_win[ni], 16)
                if 4 <= m < 8:
                    pe.wait_ge(z_dve, m - 3)
                if m >= 8:
                    pe.wait_ge(z_act, m - 7)
                for k in range(KC):
                    ins = nc.tensor.matmul(ps[4 + m % 4][:, :], hT[:, k, t * P:(t + 1) * P],
                                           win[:, k, n * BANK:(n + 1) * BANK], start=(k == 0), stop=(k == KC - 1))
                ins.then_inc(z_done, 1)
            pe.wait_ge(z_dve, 4)
            for w in range(2):
                for t in range(T):
                    for a in range(4):
                        ins = nc.tensor.transpose(ps[2 * w + t][:, a * P:(a + 1) * P],
                                                  qk[:, t, w * AW + a * P:w * AW + (a + 1) * P], ident)
                    ins.then_inc(qkT_done, 1)
            pe.wait_ge(qT_act, T)
            pe.wait_ge(kT_dve, T)
            pe.wait_ge(z_act, 6)
            for u in range(6):
                t, h0, nh, keys = unit(u)
                for i in range(nh):
                    hd = h0 + 2 * i
                    r = slice(HD * (hd % 2), HD * (hd % 2) + HD)
                    ins = nc.tensor.matmul(ps[ABANK[u]][:, i * keys:(i + 1) * keys], aqT[r, hd // 2, t * P:(t + 1) * P],
                                           akT[r, hd // 2, 0:keys], start=True, stop=True)
                ins.then_inc(sc_done, 1)
            pe.wait_ge(sgm_ok, 1)
            for t in range(T):
                pe.wait_ge(g_done, t + 1)
                for g in range(8):
                    ins = nc.tensor.matmul(ps[2 + t][:, g * 64:(g + 1) * 64], sgw[:, g * P:(g + 1) * P],
                                           zg[:, t, g * 64:(g + 1) * 64], start=True, stop=True)
                ins.then_inc(sp_done, 1)
            for u in range(6):
                pe.wait_ge(p_done, u + 1)
                if u >= 4:
                    pe.wait_ge(pT_act, u - 3)
                for a in range(4):
                    ins = nc.tensor.transpose(ps[TBANK[u]][:, a * P:(a + 1) * P], E[u][:, a * P:(a + 1) * P], ident)
                ins.then_inc(pT_done, 1)
            for t in range(T):
                pe.wait_ge(pT_act, 2 if t == 0 else 6)
                for hd in range(HEADS):
                    for kt in range(t + 1):
                        if t == 0:
                            blk = PT[hd % 2][:, (hd // 2) * P:(hd // 2 + 1) * P]
                        else:
                            b = 2 * (hd // 2 % 2) + kt
                            blk = PT[2 + hd % 2 + 2 * (hd // 4)][:, b * P:(b + 1) * P]
                        ins = nc.tensor.matmul(ps[t][:, hd * HD:(hd + 1) * HD], blk, vv[:, kt, hd * HD:(hd + 1) * HD],
                                               start=(kt == 0), stop=(kt == t))
                ins.then_inc(o_done, 1)
            for t in range(T):
                pe.wait_ge(mix_done, t + 1)
                for b in range(2):
                    for a in range(4):
                        c = 4 * b + a
                        ins = nc.tensor.transpose(ps[2 + 4 * t + b][:, a * P:(a + 1) * P], h[:, t, c * P:(c + 1) * P], ident)
                    ins.then_inc(mT_done, 1)
            pe.wait_ge(ld_wout, 16)
            for t in range(T):
                pe.wait_ge(mT_act, t + 1)
                pe.wait_ge(mT_dve, t + 1)
                for b in range(2):
                    for k in range(KC):
                        ins = nc.tensor.matmul(ps[4 + 2 * t + b][:, :], hT[:, k, t * P:(t + 1) * P],
                                               wout[:, k, b * BANK:(b + 1) * BANK], start=(k == 0), stop=(k == KC - 1))
                    ins.then_inc(wo_done, 1)
            norm_transposes(1)
            peer(0)
            norm_transposes(2)
            pe.wait_ge(b_ok, 1)
            for b in range(4):
                for a in range(4):
                    c, r = (4 * b + a) // 2, a % 2
                    ins = nc.tensor.transpose(ps[4 + b][:, a * P:(a + 1) * P],
                                              bs[:, c, r, :, :, :].rearrange("p j g n -> p (j g n)"), ident)
                ins.then_inc(bT_done, 1)
            wait_hT(2)
            pe.wait_ge(bT_act, 4)

            def s5_in(i):
                c, j = i // 4, i % 4
                if i >= 4:
                    pe.wait_ge(w_ok, i - 3)
                rows = slice(32 * j, 32 * j + 32)
                for r in range(2):
                    ins = nc.tensor.matmul(ps[i % 4][:, r * SEQ:(r + 1) * SEQ], bT[rows, 2 * c + r, :], hT[rows, c, :],
                                           start=True, stop=True)
                ins.then_inc(xs_done, 1)

            def s5_out(i):
                c, j = i // 4, i % 4
                pe.wait_ge(d_ok, 2 * (i + 1))
                if j == 0:
                    pe.wait_ge(cz_ok, 6 * (c + 1))
                    if c >= 2:
                        pe.wait_ge(ye_ok, c - 1)
                cm = [cz[:, 384 * j + P * v:384 * j + P * (v + 1)] for v in range(3)]
                d = dem[i % 2]
                for q, (m, d_) in enumerate(((cm[0], d[0][:, 0, :]), (cm[1], d[1][:, 1, :]),
                                             (cm[2], d[1][:, 0, :]), (cm[2], d[0][:, 1, :]))):
                    ins = nc.tensor.matmul(ps[4 + c % 2][:, 0:SEQ], m, d_, start=(j == 0 and q == 0),
                                           stop=(j == 3 and q == 3))
                ins.then_inc(yc_done, 1)

            s5_in(0)
            s5_in(1)
            for i in range(S5_TILES):
                if i + 2 < S5_TILES:
                    s5_in(i + 2)
                s5_out(i)
            pe.wait_ge(g_ok, 1)
            pe.wait_ge(ld_glu, 16)
            for n in range(KC):
                if n >= 2:
                    pe.wait_ge(sig_ok, n - 1)
                for k in range(KC):
                    ins = nc.tensor.matmul(ps[6 + n % 2][:, 0:SEQ], gluw[:, k, n * P:(n + 1) * P], gT[:, k, :],
                                           start=(k == 0), stop=(k == KC - 1))
                ins.then_inc(gl_done, 1)
            for t in range(T):
                pe.wait_ge(o_ok, KC)
                for b in range(2):
                    for a in range(4):
                        ins = nc.tensor.transpose(ps[2 * t + b][:, a * P:(a + 1) * P],
                                                  oT[:, 4 * b + a, t * P:(t + 1) * P], ident)
                    ins.then_inc(back_done, 1)
            norm_transposes(3)
            peer(1)

        @block.vector
        def _(dve):
            V = nc.vector

            def norm(k):
                for t in range(T):
                    dve.wait_ge(sq_done, 2 * k + t + 1)
                    V.tensor_scalar(ms[:, t:t + 1], ss[:, t:t + 1], 1.0 / D, RMS_EPS, ALU.mult, ALU.add).then_inc(ms_done, 1)
                for t in range(T):
                    dve.wait_ge(sd_done, 2 * k + t + 1)
                    V.reciprocal(rstd[:, t:t + 1], sd[:, t:t + 1])
                    dve.drain()
                    dve.wait_ge(ld_gain, 16 * (k + 1))
                    V.scalar_tensor_tensor(h[:, t, :], x[:, t, :], rstd[:, t:t + 1], gain[:, :], ALU.mult,
                                           ALU.mult).then_inc(h_done, 1)

            def norm_evac(k):
                for t in range(T):
                    dve.wait_ge(nT_done, 4 * k + 2 * t + 2)
                    V.tensor_copy(hT[:, 4:8, t * P:(t + 1) * P],
                                  ps[2 * t + 1][:, :].rearrange("p (a s) -> p a s", a=4)).then_inc(hT_dve, 1)

            def residual(t, b, bank):
                xs = x[:, t, b * BANK:(b + 1) * BANK]
                V.tensor_tensor(xs, xs, ps[bank][:, :], ALU.add).then_inc(x_done, 1)

            def peer(layer):
                for j in range(1, 8, 2):
                    dve.wait_ge(q_done, 8 * layer + j + 1)
                    V.tensor_copy(qT[:, 2 * j:2 * j + 2, :],
                                  ps[4 + j % 4][:, :].rearrange("p (a s) -> p a s", a=2)).then_inc(q_dve, 1)
                dve.wait_ge(s_act, 8 * (layer + 1))

                def route(n, par):
                    N = n + GROUPS * layer
                    V.tensor_copy(key_a[:, :, :].rearrange("p a k -> p (a k)"), S[:, bass.ds(n, 1), :].rearrange("p a k -> p (a k)"))
                    dve.drain()
                    for p in range(2):
                        V.max(top[:, p, 0:8], key_a[:, p, :])
                    dve.drain()
                    for p in range(2):
                        V.max_index(top_i[:, p, 0:8], top[:, p, 0:8], key_a[:, p, :])
                        V.match_replace(key_b[:, p, :], top[:, p, 0:8], key_a[:, p, :], LOWEST)
                    dve.drain()
                    for p in range(2):
                        V.max(top[:, p, 8:16], key_b[:, p, :])
                    dve.drain()
                    for p in range(2):
                        V.max_index(top_i[:, p, 8:16], top[:, p, 8:16], key_b[:, p, :])
                    V.tensor_tensor(cand_a[:, :].rearrange("p (a b) -> p a b", a=TOPK), bc(top[:, 0, :], [None, TOPK]),
                                    bc(top[:, 1, :], [TOPK, None]), ALU.add)
                    dve.drain()
                    V.max(cs[par][:, 0:8], cand_a[:, :])
                    V.tensor_scalar(top_f[:, 0, :], top_i[:, 0, :], float(NK * layer), None, ALU.add)
                    V.tensor_copy(top_f[:, 1, :], top_i[:, 1, :])
                    dve.drain()
                    V.max_index(pos_i[:, 0:8], cs[par][:, 0:8], cand_a[:, :])
                    V.match_replace(cand_b[:, :], cs[par][:, 0:8], cand_a[:, :], LOWEST)
                    V.tensor_scalar(ncs[par][:, :], cs[par][:, 0:1], -1.0, None, ALU.mult)
                    dve.drain()
                    V.max(cs[par][:, 8:16], cand_b[:, :])
                    dve.drain()
                    V.max_index(pos_i[:, 8:16], cs[par][:, 8:16], cand_b[:, :]).then_inc(cs_ok, 1)
                    dve.drain()
                    V.tensor_scalar(pos_ab[:, 0, :], pos_i[:, :], 4, None, ALU.logical_shift_right)
                    V.tensor_scalar(pos_ab[:, 1, :], pos_i[:, :], 15, None, ALU.bitwise_and)
                    dve.drain()
                    hot = [c[:, :].rearrange("p (a b) -> p a b", a=TOPK) for c in (cand_a, cand_b)]
                    for p in range(2):
                        V.tensor_tensor(hot[p], bc(pos_ab[:, p, :], [None, TOPK]), bc(iota16, [TOPK, None]), ALU.is_equal)
                    dve.drain()
                    for p in range(2):
                        V.tensor_tensor(hot[p], hot[p], bc(top_f[:, p, :], [TOPK, None]), ALU.mult)
                    dve.drain()
                    for p in range(2):
                        V.tensor_reduce(row[:, p, :], hot[p], AX.X, ALU.add)
                    dve.drain()
                    V.scalar_tensor_tensor(idx_all[:, bass.ds(n, 1), :].rearrange("p a k -> p (a k)"), row[:, 0, :], float(NK), row[:, 1, :], ALU.mult,
                                           ALU.add).then_inc(idx_ok, 1)

                def weigh(n, par, t):
                    N = n + GROUPS * layer
                    for s in range(TOPK):
                        dve.wait_ge(got_u[s % UR], N * 32 + 16 * (1 + s // UR))
                        V.tensor_tensor_reduce(out=ringu[:, s % UR, :], in0=ringu[:, s % UR, :], in1=h[:, t, :], scale=1.0,
                                               scalar=0.0, op0=ALU.mult, op1=ALU.add,
                                               accum_out=dots[par][:, s:s + 1]).then_inc(u_free, 1)
                    dve.wait_ge(exp_ok, N + 1)
                    V.reciprocal(grec[par][:, :], gsum[par][:, :])
                    dve.drain()
                    dve.wait_ge(gel_ok, N + 1)
                    V.scalar_tensor_tensor(wgt[par][:, :], gexp[par][:, :], grec[par][:, :], gel[par][:, :], ALU.mult, ALU.mult)
                    dve.drain()
                    dve.wait_ge(v_free, N * 16 + 16)
                    V.tensor_tensor(diag[par], bc(ident, [TOPK, None]), bc(wgt[par][:, :], [None, P]),
                                    ALU.mult).then_inc(diag_ok, 1)

                route(0, 0)
                for t in range(T):
                    loops = PH // 2 - (t == T - 1)
                    with dve.Fori(0, loops) as it:
                        n = it * 2 + PH * t
                        route(n + 1, 1)
                        weigh(n, 0, t)
                        route(n + 2, 0)
                        weigh(n + 1, 1, t)
                route(GROUPS - 1, 1)
                weigh(GROUPS - 2, 0, T - 1)
                weigh(GROUPS - 1, 1, T - 1)
                for t in range(T):
                    dve.wait_ge(y_done, 2 * layer + t + 1)
                    for b in range(2):
                        residual(t, b, 4 + 2 * t + b)

            V.memset(zeros[:, :], 0.0).then_inc(zero_ok, 1)
            V.memset(rden[:, 0:1], 0.0).then_inc(u_free, UR)
            V.memset(rden[:, 1:2], 0.0).then_inc(v_free, 2 * VR)
            norm(0)
            norm_evac(0)
            for m in range(4):
                w, t = m // 2, m % 2
                dve.wait_ge(z_done, m + 1)
                z4 = ps[4 + m][:, :].rearrange("p (h a d) -> p h a d", h=HEADS, a=2)
                a4 = rot_a.rearrange("p (h a d) -> p h a d", h=HEADS, a=2)
                b4 = rot_b.rearrange("p (h a d) -> p h a d", h=HEADS, a=2)
                V.tensor_tensor(a4, z4, bc(cos_t[:, t, :], [HEADS, 2, None]), ALU.mult)
                V.tensor_tensor(b4[:, :, 0, :], z4[:, :, 1, :], bc(nsin_t[:, t, :], [HEADS, None]), ALU.mult)
                V.tensor_tensor(b4[:, :, 1, :], z4[:, :, 0, :], bc(sin_t[:, t, :], [HEADS, None]), ALU.mult)
                dve.drain()
                V.tensor_tensor(qk[:, t, w * AW:(w + 1) * AW], rot_a, rot_b, ALU.add).then_inc(z_dve, 1)
                dve.drain()
            dve.wait_ge(dt_ok, 1)
            V.tensor_tensor(th, lam_i, dt_, ALU.mult)
            V.tensor_tensor(lrdt, lam_r, dt_, ALU.mult).then_inc(th_ok, 1)
            dve.drain()
            V.tensor_scalar(kf, th, INV_TWO_PI, ROUND, ALU.mult, ALU.add)
            dve.drain()
            V.tensor_scalar(kf, kf, ROUND, None, ALU.subtract)
            dve.drain()
            V.scalar_tensor_tensor(th, kf, -TWO_PI_HI, th, ALU.mult, ALU.add)
            dve.drain()
            V.scalar_tensor_tensor(th, kf, -TWO_PI_LO, th, ALU.mult, ALU.add)
            dve.drain()
            V.tensor_scalar(th, th, PI_BELOW, -PI_BELOW, ALU.min, ALU.max).then_inc(thr_ok, 1)
            dve.drain()
            V.tensor_scalar(thp, th, INV_TWO_PI, None, ALU.mult)
            for t in range(T):
                dve.wait_ge(z_act, 3 + t)
                g3 = zg[:, t, :].rearrange("p (g d) -> p g d", g=8)
                s3 = sg_tmp.rearrange("p (g d) -> p g d", g=8)
                V.tensor_reduce(mu[:, :], g3, AX.X, ALU.add)
                dve.drain()
                V.scalar_tensor_tensor(g3, bc(mu[:, :], [None, 64]), -1.0 / 64, g3, ALU.mult, ALU.add)
                dve.drain()
                V.tensor_tensor(s3, g3, g3, ALU.mult)
                dve.drain()
                V.tensor_reduce(var[:, :], s3, AX.X, ALU.add)
                dve.drain()
                V.tensor_scalar(var[:, :], var[:, :], 1.0 / 64, LN_EPS, ALU.mult, ALU.add).then_inc(lnv_done, 1)
                if t == 0:
                    for t2 in range(T):
                        dve.wait_ge(qkT_done, T + t2 + 1)
                        V.tensor_copy(akT[:, :, t2 * P:(t2 + 1) * P],
                                      ps[2 + t2][:, :].rearrange("p (a s) -> p a s", a=4)).then_inc(kT_dve, 1)
                dve.wait_ge(lsd_done, t + 1)
                V.reciprocal(lrs[:, :], lsd[:, :])
                dve.drain()
                V.tensor_tensor(g3, g3, bc(lrs[:, :], [None, 64]), ALU.mult)
                dve.drain()
                if t == 0:
                    dve.wait_ge(ld_sgu, 48)
                V.tensor_tensor(zg[:, t, :], zg[:, t, :], sg_gain, ALU.mult).then_inc(g_done, 1)
                dve.drain()
            for u in range(6):
                t, h0, nh, keys = unit(u)
                dve.wait_ge(sc_done, u + 1)
                e3 = E[u].rearrange("p (h k) -> p h k", h=nh)
                V.scalar_tensor_tensor(e3, ps[ABANK[u]][:, :].rearrange("p (h k) -> p h k", h=nh), SCALE,
                                       bc(negm[t], [nh, None]), ALU.mult, ALU.add)
                dve.drain()
                V.tensor_reduce(negmax[:, 8 * t + h0:8 * t + h0 + 2 * nh - 1:2], e3, AX.X, ALU.max, negate=True).then_inc(nm_done, 1)
            for u in range(6):
                t, h0, nh, keys = unit(u)
                dve.wait_ge(ex_done, u + 1)
                e3 = E[u].rearrange("p (h k) -> p h k", h=nh)
                V.tensor_tensor(e3, e3, bc(count[t], [nh, None]), ALU.mult)
                dve.drain()
                V.tensor_reduce(den[:, 8 * t + h0:8 * t + h0 + 2 * nh - 1:2], e3, AX.X, ALU.add).then_inc(p_done, 1)
            dve.drain()
            V.reciprocal(rden[:, :], den[:, :])
            dve.drain()
            for t in range(T):
                dve.wait_ge(sp_done, t + 1)
                dve.wait_ge(z_act, 6)
                s3 = sg_tmp.rearrange("p (g d) -> p g d", g=8)
                V.tensor_tensor(s3, ps[2 + t][:, :].rearrange("p (g d) -> p g d", g=8), bc(sgb[:, :], [None, 64]), ALU.add)
                dve.drain()
                V.tensor_tensor(h[:, t, AW:2 * AW], sg_tmp, zu[:, t, :], ALU.mult)
                dve.drain()
            for t in range(T):
                dve.wait_ge(o_done, t + 1)
                V.tensor_tensor(h[:, t, 0:AW].rearrange("p (h d) -> p h d", h=HEADS),
                                ps[t][:, :].rearrange("p (h d) -> p h d", h=HEADS),
                                bc(rden[:, 8 * t:8 * t + 8], [None, HD]), ALU.mult).then_inc(mix_done, 1)
            for t in range(T):
                dve.wait_ge(mT_done, 2 * t + 2)
                V.tensor_copy(hT[:, 4:8, t * P:(t + 1) * P],
                              ps[3 + 4 * t][:, :].rearrange("p (a s) -> p a s", a=4)).then_inc(mT_dve, 1)
            for t in range(T):
                for b in range(2):
                    dve.wait_ge(wo_done, 2 * t + b + 1)
                    residual(t, b, 4 + 2 * t + b)
            dve.wait_ge(cs5_ok, 1)
            dve.wait_ge(dec_ok, 1)
            V.tensor_tensor(ar, dec, cs_, ALU.mult)
            V.tensor_tensor(ai, dec, sn_, ALU.mult)
            V.tensor_tensor(mag, lam_r, lam_r, ALU.mult)
            V.tensor_tensor(kf, lam_i, lam_i, ALU.mult)
            dve.drain()
            V.tensor_tensor(mag, mag, kf, ALU.add)
            V.tensor_scalar(ar, ar, 1.0, None, ALU.subtract)
            dve.drain()
            V.reciprocal(mag, mag)
            V.tensor_tensor(kr, ar, lam_r, ALU.mult)
            V.tensor_tensor(kf, ai, lam_i, ALU.mult)
            V.tensor_tensor(ki, ai, lam_r, ALU.mult)
            V.tensor_tensor(ab, ar, lam_i, ALU.mult)
            dve.drain()
            V.tensor_tensor(kr, kr, kf, ALU.add)
            V.tensor_tensor(ki, ki, ab, ALU.subtract)
            dve.drain()
            V.tensor_tensor(kr, kr, mag, ALU.mult)
            V.tensor_tensor(ki, ki, mag, ALU.mult)
            norm(1)
            norm_evac(1)
            peer(0)
            norm(2)
            norm_evac(2)
            V.memset(bs, 0.0)
            dve.wait_ge(ld_b, 16)
            for r in range(2):
                for dst, k_, r_ in ((bt1, kr, r), (bt2, ki, 1 - r)):
                    V.tensor_tensor(dst.rearrange("p (i n) -> p i n", i=S5_TILES), bc(k_, [None, 16]),
                                    b_raw[:, r_, :].rearrange("p (i n) -> p i n", i=S5_TILES), ALU.mult)
                dve.drain()
                for g in range(2):
                    half = slice(64 * g, 64 * g + 64)
                    ins = V.tensor_tensor(bs[half, :, r, :, g, :], bt1[half, :].rearrange("p (c j n) -> p c j n", c=8, j=4),
                                          bt2[half, :].rearrange("p (c j n) -> p c j n", c=8, j=4),
                                          (ALU.subtract, ALU.add)[r])
                dve.drain()
            ins.then_inc(b_ok, 1)

            def skip(c):
                dve.wait_ge(yc_done, 4 * (c + 1))
                V.scalar_tensor_tensor(gT[:, c, :], hT[:, c, :], dskip[:, c:c + 1], ps[4 + c % 2][:, 0:SEQ], ALU.mult,
                                       ALU.add).then_inc(ye_ok, 1)

            for i in range(S5_TILES):
                c, j = i // 4, i % 4
                dve.wait_ge(xs_done, i + 1)
                dve.wait_ge(tab_ok, c + 1)
                x3 = ps[i % 4][:, :].rearrange("p (r s) -> p r s", r=2)
                V.tensor_tensor(prod[0], x3, bc(tab[c % 2][:, 0, j, :], [2, None]), ALU.mult)
                V.tensor_tensor(prod[1], x3, bc(tab[c % 2][:, 1, j, :], [2, None]), ALU.mult)
                dve.drain()
                V.tensor_tensor(prod[0][:, 0, :], prod[0][:, 0, :], prod[1][:, 1, :], ALU.add)
                V.tensor_tensor(prod[0][:, 1, :], prod[0][:, 1, :], prod[1][:, 0, :], ALU.subtract).then_inc(w_ok, 1)
                dve.drain()
                if i >= 2:
                    dve.wait_ge(d_ok, 2 * (i - 1))
                for r in range(2):
                    V.tensor_tensor_scan(zst[i % 2][:, r, :], dec[:, i:i + 1].to_broadcast([P, SEQ]),
                                         prod[0][:, r, :], 0.0, ALU.mult, ALU.add).then_inc(st_ok, 1)
                dve.drain()
                if j == 2 and c >= 1:
                    skip(c - 1)
            skip(KC - 1)
            for n in range(KC):
                dve.wait_ge(sig_ok, n + 1)
                V.tensor_tensor(oT[:, n, :], sig[:, n, :], gT[:, n, :], ALU.mult).then_inc(o_ok, 1)
            for t in range(T):
                for b in range(2):
                    dve.wait_ge(back_done, 2 * t + b + 1)
                    residual(t, b, 2 * t + b)
            norm(3)
            norm_evac(3)
            peer(1)
            norm(4)


def constants():
    import numpy as np
    c = np.zeros((P, C_ALL), np.float32)
    c[:, C_ID:C_ID + P] = np.eye(P, dtype=np.float32)
    tok = np.arange(SEQ)
    d = tok[:, None] - tok[None, :]
    cnt = ((d >= 0) & (d <= 128)).astype(np.float32)
    for window, dil in ((512, 4), (2048, 16)):
        cnt += ((d >= 0) & (d <= window) & (d % dil == 0)).astype(np.float32)
    neg = np.where(cnt > 0, np.float32(0), np.float32(-1e37))
    half = HD // 2
    inv = np.power(np.float32(10000.0), (-2.0 * np.arange(half, dtype=np.float32) / HD).astype(np.float32))
    ang = tok.astype(np.float32)[:, None] * inv.astype(np.float32)[None, :]
    for t in range(T):
        r = slice(t * P, (t + 1) * P)
        keys = P * (t + 1)
        c[:, C_CNT + P * t:C_CNT + P * t + keys] = cnt[r, :keys]
        c[:, C_NEG + P * t:C_NEG + P * t + keys] = neg[r, :keys]
        c[:, C_COS + half * t:C_COS + half * (t + 1)] = np.cos(ang[r])
        c[:, C_SIN + half * t:C_SIN + half * (t + 1)] = np.sin(ang[r])
        c[:, C_NSIN + half * t:C_NSIN + half * (t + 1)] = -np.sin(ang[r])
    c[:, C_IOTA:C_IOTA + 16] = np.arange(16)
    c[:, C_TIME:C_TIME + SEQ] = np.arange(SEQ)
    c[:, C_HPI] = np.pi / 2
    return c


def kernel(x, norm_mix_g, norm_ffn_g, final_norm_g, mix_w_in, sgu_norm_g, sgu_w, sgu_b, mix_w_out, s5_lambda_re,
           s5_lambda_im, s5_b_re, s5_b_im, s5_c_re, s5_c_im, s5_d, s5_log_step, glu_w, glu_b, peer_wq, peer_subkeys,
           peer_u, peer_v):
    import numpy as np
    import concourse.bacc as bacc
    from concourse.bass_utils import run_bass_kernel_spmd as run

    a = np.asarray

    def states(v):
        v = a(v)
        v = v.reshape((32, 2, 64) + v.shape[2:])
        return v.transpose((1, 2, 0) + tuple(range(3, v.ndim))).reshape((P, 32) + v.shape[3:])

    def columns(v):
        return a(v).reshape(KC, P).T

    log_step = np.broadcast_to(a(s5_log_step)[0][:, None], (64, 64))
    data = {
        "x": a(x).reshape(SEQ, D),
        "gains": np.stack([a(norm_mix_g)[0], a(norm_ffn_g)[0], a(norm_mix_g)[1], a(norm_ffn_g)[1], a(final_norm_g)]),
        "cst": constants(),
        "w_in": a(mix_w_in)[0],
        "sgu_g": a(sgu_norm_g)[0].reshape(1, AW),
        "sgu_wT": a(sgu_w)[0].transpose(2, 0, 1).reshape(P, 8 * P),
        "sgu_bT": a(sgu_b)[0].T,
        "w_out": a(mix_w_out)[0],
        "s5_par": np.concatenate([states(a(s5_lambda_re)[0]), states(a(s5_lambda_im)[0]), states(log_step)], axis=1),
        "s5_b": np.stack([states(a(s5_b_re)[0]).reshape(P, 512), states(a(s5_b_im)[0]).reshape(P, 512)], axis=1),
        "s5_c": np.stack([states(a(s5_c_re)[0].transpose(0, 2, 1)), states(a(s5_c_im)[0].transpose(0, 2, 1))], axis=1),
        "s5_dv": columns(a(s5_d)[0]),
        "glu_bv": columns(a(glu_b)[0]),
        "glu_w": a(glu_w)[0],
        "wq": a(peer_wq),
        "skT": a(peer_subkeys).transpose(3, 0, 1, 2),
        "u_tab": a(peer_u).reshape(2 * EXPERTS, D),
        "v_tab": a(peer_v).reshape(2 * EXPERTS, D),
    }
    nc = bacc.Bacc("TRN2", target_bir_lowering=False, num_devices=1)
    arrays, args = {}, []
    for name, v in data.items():
        v = np.ascontiguousarray(v)
        arrays[f"in_{name}_dram"] = v
        args.append(nc.dram_tensor(f"in_{name}_dram", v.shape, mybir.dt.from_np(v.dtype), kind="ExternalInput").ap())
    args.append(nc.dram_tensor("out_0_dram", (SEQ, D), F32, kind="ExternalOutput").ap())
    trunk(nc, *args)
    r = run(nc, [arrays], core_ids=[0])
    return r.results[0]["out_0_dram"].reshape(1, SEQ, D)
```

```python
import math
from contextlib import ExitStack

import concourse.bass as bass
from concourse import mybir

ALU = mybir.AluOpType
ACT = mybir.ActivationFunctionType
AX = mybir.AxisListType
F32 = mybir.dt.float32
U32 = mybir.dt.uint32

P = 128
SEQ = 256
D = 1024
T = SEQ // P
KC = D // P
HEADS, HD = 8, 64
AW = HEADS * HD
BANK = 512
PH, NK, TOPK = 8, 128, 16
EXPERTS = NK * NK
GROUPS = 2 * T * PH
RING = 8
S5_TILES = 32
RMS_EPS, LN_EPS = 1e-6, 1e-5
SCALE = HD ** -0.5
LOWEST = -3.0e38
ROUND = 12582912.0
TWO_PI_HI = 6.28125
TWO_PI_LO = 2 * math.pi - 6.28125
INV_TWO_PI = 1 / (2 * math.pi)
TURN = 6.2831845
PI_BELOW = 3.1415925

NORM_T = [0, 1, 0, 1, 0, 0, 1, 1, 0, 1]
NORM_VEC = [0, 0, 1, 1, 2, 5, 6, 9, 10, 10]
VEC_ROW = [0, 1, 2, 5, 6, 3, 2, 5, 6, 3, 4]
D_VEC, BIAS_VEC = [3, 7], [4, 8]
WOUT_BLK = [0, 6]
GLU_BLK = [12, 18]
Q_BLK = [2, 8, 14, 20]
Q_NORM = [2, 3, 5, 7]
Z_ORDER = [(0, 0), (0, 1), (0, 2), (0, 4), (0, 3), (1, 0), (1, 1), (1, 2), (1, 4), (1, 3)]

PRELUDE = [("norm", 0), ("z", 0), ("z", 1), ("norm", 1), ("z", 2), ("z", 3), ("z", 4), ("s5_angle",), ("qk_turn", 0),
           ("att_a", 0), ("sgu_a", 0), ("z", 5), ("att_b", 0), ("sgu_b", 0), ("mix", 0), ("z", 6), ("w_out", 0),
           ("z", 7), ("norm", 2), ("z", 8), ("z", 9), ("qk_turn", 1), ("query", 0, 0), ("query", 0, 2), ("scores", 0)]


def between():
    work = {n: [] for n in range(GROUPS)}
    work[0] = [("sgu_a", 1), ("att_a", 1), ("att_b", 1)]
    work[1] = [("att_a", 2), ("att_b", 2)]
    work[2] = [("sgu_b", 1), ("mix", 1)]
    work[3] = [("w_out", 1), ("norm", 3)]
    work[4] = [("query", 1, 0)]
    work[5] = [("query", 1, 2)]
    work[6] = [("scores", 1)]
    work[7] = [("s5_setup",)]
    for t in range(T):
        g = 8 * (t + 1)
        work[g] = [("y_sum", 2 + 2 * t), ("norm", 4 + 2 * t)]
        work[g + 1] = [("s5", t, 0), ("s5", t, 1), ("s5", t, 2)]
        work[g + 2] = [("s5", t, 3), ("s5", t, 4), ("s5", t, 5)]
        work[g + 3] = [("s5", t, 6), ("s5", t, 7), ("s5_end", t)]
        work[g + 4] = [("glu", t), ("norm", 5 + 2 * t)]
        work[g + 5] = [("query", 2 + t, 0)]
        work[g + 6] = [("query", 2 + t, 2), ("scores", 2 + t)]
    work[24] = [("y_sum", 6), ("norm", 8)]
    return work


WORK = between()
LAST = [("y_sum", 7), ("norm", 9)]

C_ID, C_CNT, C_NEG, C_COS, C_SIN, C_NSIN, C_IOTA, C_TIME, C_HPI = 0, 128, 512, 896, 960, 1024, 1088, 1104, 1232
C_ALL = 1233


def trunk(nc, x_in, vecs, cst_in, w_in, sgu_g, sgu_wT, sgu_bT, w_out, s5_par, s5_b, s5_c, glu_w, wq, skT, u_tab, v_tab,
          out):
    with ExitStack() as ctx:
        def sb(name, shape, dt=F32):
            return ctx.enter_context(nc.sbuf_tensor(name, shape, dt))

        def sem(name):
            return ctx.enter_context(nc.semaphore(name))

        x = sb("x", [P, T, D])
        h = sb("h", [P, T, D])
        hT = sb("hT", [P, KC, P])
        cst = sb("cst", [P, C_ALL])
        vec = sb("vec", [P, 2, D])
        sk = sb("sk", [P, 2, 2, NK])
        ss, ms, sd, rstd = (sb(n, [P, T]) for n in ("ss", "ms", "sd", "rstd"))
        rings = sb("rings", [P, 2 * RING * D])
        wst = sb("wst", [P, 2, KC, BANK])
        mem = sb("mem", [P, 9216])
        dgs = sb("dgs", [P, 2 * TOPK * P])
        scr = sb("scr", [P, 2048])
        sgw = sb("sgw", [P, D])
        ps = ctx.enter_context(nc.psum_tensor("ps", [P, 8, BANK], F32))

        def four(bank):
            return ps[:, bank, :].rearrange("p (a s) -> p a s", a=4)

        ident = cst[:, C_ID:C_ID + P]
        count = [cst[:, C_CNT + P * t:C_CNT + P * (2 * t + 1)] for t in range(T)]
        negm = [cst[:, C_NEG + P * t:C_NEG + P * (2 * t + 1)] for t in range(T)]
        cos_t = cst[:, C_COS:C_COS + 64].rearrange("p (t k) -> p t k", t=T)
        sin_t = cst[:, C_SIN:C_SIN + 64].rearrange("p (t k) -> p t k", t=T)
        nsin_t = cst[:, C_NSIN:C_NSIN + 64].rearrange("p (t k) -> p t k", t=T)
        iota16 = cst[:, C_IOTA:C_IOTA + 16]
        time_row = cst[:, C_TIME:C_TIME + P]
        half_pi = cst[:, C_HPI:C_HPI + 1]

        win = [rings[:, 4096 * i:4096 * (i + 1)] for i in range(3)] + [dgs[:, :], rings[:, 12288:16384]]
        win = [w.rearrange("p (k n) -> p k n", k=KC) for w in win]
        hT1 = scr[:, 0:1024].rearrange("p (k s) -> p k s", k=KC)
        qk = [scr[:, 1024 + BANK * w:1536 + BANK * w] for w in range(2)]

        def part(start, size, pattern="p (a s) -> p a s", **dims):
            ap = mem[:, start:start + size]
            return ap.rearrange(pattern, **dims) if dims else ap

        akT, aqT = part(0, 1024, a=4), part(1024, 1024, a=4)
        vv, zu, zg = (part(2048 + 1024 * i, 1024, a=T) for i in range(3))
        E = [part(5120 + BANK * i, BANK) for i in range(2)]
        PT = [part(6144 + BANK * i, BANK) for i in range(2)]
        sg_tmp, sg_gain, rot_a, rot_b = (part(7168 + BANK * i, BANK) for i in range(4))
        negmax, den, rden = (sb(n, [P, 16]) for n in ("negmax", "den", "rden"))
        mu, var, lsd, lrs = (sb(n, [P, 8]) for n in ("mu", "var", "lsd", "lrs"))
        sgb = sb("sgb", [P, 8])

        ringu = rings[:, 0:RING * D].rearrange("p (b n) -> p b n", b=RING)
        ringv = rings[:, RING * D:].rearrange("p (b n) -> p b n", b=RING)
        qs = [[dgs[:, 2048 + BANK * i:2048 + BANK * (i + 1)] for i in range(2)]] + [
            [part(4864 + BANK * i, BANK) for i in range(2)]] * 3
        qT = [dgs[:, 0:2048].rearrange("p (a s) -> p a s", a=16)] + [part(2816, 2048, a=16)] * 3
        S = scr[:, :].rearrange("p (g k) -> p g k", g=PH)
        diag = [dgs[:, 2048 * i:2048 * (i + 1)].rearrange("p (s t) -> p s t", s=TOPK) for i in range(2)]
        key_b = sb("key_b", [P, 2, NK])
        cand_a, cand_b = sb("cand_a", [P, 256]), sb("cand_b", [P, 256])
        top = sb("top", [P, 2, TOPK])
        top_i = sb("top_i", [P, 2, TOPK], U32)
        top_f = sb("top_f", [P, 2, TOPK])
        pos_i = sb("pos_i", [P, TOPK], U32)
        pos_ab = sb("pos_ab", [P, 2, TOPK], U32)
        row = sb("row", [P, 2, TOPK])
        idx = [sb(f"idx{i}", [P, TOPK], U32) for i in range(4)]
        cs, gexp, dots, gel, wgt = ([sb(f"{n}{i}", [P, TOPK]) for i in range(2)] for n in ("cs", "gexp", "dots", "gel", "wgt"))
        ncs, gsum, grec = ([sb(f"{n}{i}", [P, 1]) for i in range(2)] for n in ("ncs", "gsum", "grec"))

        s5p = sb("s5p", [P, 3 * S5_TILES])
        lam_r, lam_i, log_step = (s5p[:, S5_TILES * i:S5_TILES * (i + 1)] for i in range(3))
        s5s = sb("s5s", [P, 16, S5_TILES])
        (dt_, lrdt, th, dec, kf, ab, sn_, cs_, ar, ai, mag, kr, ki, thp, cos_n, sin_n) = (s5s[:, i, :] for i in range(16))
        z_last, z_init = sb("z_last", [P, S5_TILES, 2]), sb("z_init", [P, 2, S5_TILES])
        bT = part(0, 2048, a=16)
        cmat = [part(2048 + 384 * i, 384, "p (j v n) -> p j v n", j=4, v=3) for i in range(2)]
        tab = [part(2816 + 1024 * i, 1024, "p (r j s) -> p r j s", r=2, j=4) for i in range(2)]
        turns, whole = part(4864, 512, a=4), part(5376, 512, a=4)
        prod = [[part(5888 + 1024 * i + 512 * v, 512, "p (i r s) -> p i r s", i=2, r=2) for v in range(2)] for i in range(2)]
        zst = part(7936, 512, "p (i r s) -> p i r s", i=2, r=2)
        bs = part(2816, 2048, "p (c r j g n) -> p c r j g n", c=8, r=2, j=4, g=2)
        b_raw = part(4864, 1024, a=2)
        bt1, bt2 = part(5888, 512), part(6400, 512)
        c_raw = sgw[:, :].rearrange("p (r i n) -> p r i n", r=2, i=S5_TILES)
        gate = part(2816, 1024)

        ld_x = [sem(f"ld_x{t}") for t in range(T)]
        ld_cst, ld_sgu, ld_sk, ld_s5, ld_c, ld_b, st_out = (
            sem(n) for n in ("ld_cst", "ld_sgu", "ld_sk", "ld_s5", "ld_c", "ld_b", "st_out"))
        ld_win = [sem(f"ld_win{n}") for n in range(5)]
        ld_w = [sem(f"ld_w{i}") for i in range(2)]
        ld_vec = [sem(f"ld_vec{i}") for i in range(2)]
        got_u = [sem(f"got_u{b}") for b in range(RING)]
        got_v = [sem(f"got_v{b}") for b in range(RING)]
        sq_done, ms_done, sd_done, h_done, nT_done, hT_act, hT_dve, x_done, w_used = (sem(n) for n in (
            "sq_done", "ms_done", "sd_done", "h_done", "nT_done", "hT_act", "hT_dve", "x_done", "w_used"))
        (z_done, z_dve, z_act, sgm_ok, qkT_done, qT_act, kT_dve, lnv_done, lsd_done, g_done, sc_done, nm_done, ex_done,
         p_done, pT_done, pT_act, sp_done, o_done, mix_done, mT_done, mT_act, mT_dve) = (sem(n) for n in (
             "z_done", "z_dve", "z_act", "sgm_ok", "qkT_done", "qT_act", "kT_dve", "lnv_done", "lsd_done", "g_done",
             "sc_done", "nm_done", "ex_done", "p_done", "pT_done", "pT_act", "sp_done", "o_done", "mix_done",
             "mT_done", "mT_act", "mT_dve"))
        (qs_act, qt_done, qt_dve, s_done, s_act, idx_ok, cs_ok, exp_ok, u_free, v_free, gel_ok, diag_ok, y_done) = (
            sem(n) for n in ("qs_act", "qt_done", "qt_dve", "s_done", "s_act", "idx_ok", "cs_ok", "exp_ok", "u_free",
                             "v_free", "gel_ok", "diag_ok", "y_done"))
        (dt_ok, th_ok, dec_ok, thr_ok, cs5_ok, n_ok, csn_ok, b_ok, bT_done, bT_act, whole_ok, frac_ok, tab_ok, xs_done,
         w_ok, d_ok, cz_zero, cz_ok, yc_done, dh_done, ye_ok, g_ok, gT_done, gT_act, gT_dve, bias_ok, sig_ok) = (
             sem(n) for n in (
                 "dt_ok", "th_ok", "dec_ok", "thr_ok", "cs5_ok", "n_ok", "csn_ok", "b_ok", "bT_done", "bT_act",
                 "whole_ok", "frac_ok", "tab_ok", "xs_done", "w_ok", "d_ok", "cz_zero", "cz_ok", "yc_done", "dh_done",
                 "ye_ok", "g_ok", "gT_done", "gT_act", "gT_dve", "bias_ok", "sig_ok"))

        block = ctx.enter_context(nc.Block())

        def att_units(a):
            return (0, [(0, 4), (1, 4)]) if a == 0 else (1, [(4 * a - 4, 2), (4 * a - 3, 2)])

        def bc(ap, dims):
            at = dims.index(None)
            for _ in range(at):
                ap = ap.unsqueeze(1)
            for _ in range(len(dims) - 1 - at):
                ap = ap.unsqueeze(len(ap.shape))
            return ap.to_broadcast([ap.shape[0]] + [ap.shape[1 + at] if d is None else d for d in dims])

        def z_evacs(zi, on_dve):
            return sum((n < 2) == on_dve for _, n in Z_ORDER[:zi])

        def hT_of(m):
            return hT1 if m == 1 else hT

        @block.sync
        def _(sp):
            vec_read = {0: (h_done, 2), 1: (h_done, 4), 2: (h_done, 5), 3: (dh_done, 1), 4: (bias_ok, 2), 5: (h_done, 6),
                        6: (h_done, 7), 7: (dh_done, 2), 8: (bias_ok, 4)}

            def load_vec(v):
                if v >= 2:
                    sp.wait_ge(*vec_read[v - 2])
                r = VEC_ROW[v]
                sp.dma_start(vec[:, v % 2, :], vecs[r:r + 1, :].to_broadcast([P, D])).then_inc(ld_vec[v % 2], 16)

            blocks = []
            for b, mats in ((0, (w_out, 2)), (0, (wq[0], 4)), (0, (w_out, 2)), (0, (wq[0], 4)), (0, (glu_w, 2)),
                            (0, (wq[1], 4)), (0, (glu_w, 2)), (0, (wq[1], 4))):
                blocks += [(mats[0], n) for n in range(mats[1])]

            def load_w(*which):
                for w in which:
                    if w >= 2:
                        sp.wait_ge(w_used, w - 1)
                    m, n = blocks[w]
                    sp.dma_start(wst[:, w % 2, :, :], m.rearrange("(k p) n -> p k n", p=P)[:, :, n * BANK:(n + 1) * BANK])\
                        .then_inc(ld_w[w % 2], 16)

            w_v = w_in.rearrange("(k p) n -> p k n", p=P)

            def load_win(n):
                sp.dma_start(win[n], w_v[:, :, n * BANK:(n + 1) * BANK]).then_inc(ld_win[n], 16)

            sp.dma_start(x[:, 0, :], x_in[0:P, :]).then_inc(ld_x[0], 16)
            load_vec(0)
            sp.dma_start(cst[:, :], cst_in).then_inc(ld_cst, 16)
            load_win(0)
            load_win(1)
            sp.dma_start(x[:, 1, :], x_in[P:2 * P, :]).then_inc(ld_x[1], 16)
            load_win(2)
            load_win(4)
            load_win(3)
            sp.dma_start(sgw[:, :], sgu_wT).then_inc(ld_sgu, 16)
            sp.dma_start(sg_gain, sgu_g.to_broadcast([P, AW])).then_inc(ld_sgu, 16)
            sp.dma_start(sgb[:, :], sgu_bT).then_inc(ld_sgu, 16)
            sp.dma_start(s5p[:, :], s5_par).then_inc(ld_s5, 16)
            load_w(0, 1)
            load_vec(1)
            sp.dma_start(sk[:, :, :, :], skT).then_inc(ld_sk, 16)
            load_w(2, 3, 4, 5, 6, 7)
            load_vec(2)
            sp.wait_ge(sp_done, T)
            sp.dma_start(c_raw, s5_c).then_inc(ld_c, 16)
            load_w(8, 9)
            load_vec(3)
            load_w(10, 11)
            sp.wait_ge(s_done, 8)
            sp.dma_start(b_raw, s5_b).then_inc(ld_b, 16)
            load_w(12, 13)
            load_vec(4)
            load_vec(5)
            load_w(14, 15)
            load_vec(6)
            load_vec(7)
            load_w(16, 17, 18, 19)
            load_vec(8)
            load_vec(9)
            load_w(20, 21)
            load_vec(10)
            load_w(22, 23)
            for t in range(T):
                sp.wait_ge(h_done, 9 + t)
                sp.dma_start(out[t * P:(t + 1) * P, :], h[:, t, :]).then_inc(st_out, 16)
            sp.wait_ge(st_out, 16 * T)

        @block.gpsimd
        def _(pool):
            pool.wait_ge(ld_sgu, 48)
            sg3 = sgw[:, :].rearrange("p (h i) -> p h i", h=8)
            nc.gpsimd.affine_select(out=sg3, in_=sg3, pattern=[[0, 8], [1, P]], compare_op=ALU.is_ge, fill=0.0, base=0,
                                    channel_multiplier=-1).then_inc(sgm_ok, 1)

            def gather(ring, table, window, s, done):
                nc.gpsimd.indirect_dma_start(
                    out=ring[:, s % RING, :], out_offset=None, in_=table,
                    in_offset=bass.IndirectOffsetOnAxis(ap=idx[window][:, s:s + 1], axis=0)).then_inc(done[s % RING], 16)

            def gathers(n, q, last=False):
                if not last:
                    pool.wait_ge(idx_ok, n + 2)
                for s in range(TOPK):
                    if s % 2 == 0:
                        pool.wait_ge(v_free, n * 16 + (s + 2))
                        if not last:
                            pool.wait_ge(u_free, n * 16 + (s + 18))
                        pool.nop(nofuse=True)
                    gather(ringv, v_tab, q, s, got_v)
                    if not last:
                        gather(ringu, u_tab, (q + 1) % 4, s, got_u)

            pool.wait_ge(idx_ok, 1)
            pool.wait_ge(z_done, len(Z_ORDER))
            for s in range(TOPK):
                if s >= RING and s % 2 == 0:
                    pool.wait_ge(u_free, s + 2)
                gather(ringu, u_tab, 0, s, got_u)
            with pool.Fori(0, GROUPS // 4 - 1) as it:
                for q in range(4):
                    gathers(it * 4 + q, q)
            for q in range(4):
                gathers(GROUPS - 4 + q, q, last=(q == 3))

        @block.scalar
        def _(act):
            A = nc.scalar

            def norm(m):
                t = NORM_T[m]
                if m < 2:
                    act.wait_ge(ld_x[t], 16)
                else:
                    act.wait_ge(x_done, 2 * (m - 1))
                A.activation(h[:, t, :], x[:, t, :], ACT.Square, accum_out=ss[:, t:t + 1]).then_inc(sq_done, 1)
                act.wait_ge(ms_done, m + 1)
                A.activation(sd[:, t:t + 1], ms[:, t:t + 1], ACT.Sqrt).then_inc(sd_done, 1)
                if m < 8:
                    act.wait_ge(nT_done, 2 * m + 1)
                    A.activation(hT_of(m)[:, 0:4, :], four(0), ACT.Copy).then_inc(hT_act, 1)

            def z(zi):
                t, n = Z_ORDER[zi]
                if n >= 2:
                    act.wait_ge(z_done, zi + 1)
                    dst, fn = {2: (vv, ACT.Copy), 3: (zu, ACT.Gelu_apprx_tanh), 4: (zg, ACT.Gelu_apprx_tanh)}[n]
                    A.activation(dst[:, t, :], ps[:, 4 + zi % 2, :], fn).then_inc(z_act, 1)

            def s5_angle():
                act.wait_ge(ld_s5, 16)
                A.activation(dt_, log_step, ACT.Exp).then_inc(dt_ok, 1)
                act.wait_ge(th_ok, 1)
                A.activation(dec, lrdt, ACT.Exp).then_inc(dec_ok, 1)

            def qk_turn(t):
                act.wait_ge(qkT_done, 2 * t + 1)
                A.activation(aqT[:, :, t * P:(t + 1) * P], four(2), ACT.Copy).then_inc(qT_act, 1)

            def att_a(a):
                t, units = att_units(a)
                keys = P * (t + 1)
                for i, (h0, nh) in enumerate(units):
                    act.wait_ge(nm_done, 2 * a + i + 1)
                    for j in range(nh):
                        c = 8 * t + h0 + 2 * j
                        e = E[i][:, j * keys:(j + 1) * keys]
                        ins = A.activation(e, e, ACT.Exp, bias=negmax[:, c:c + 1])
                    ins.then_inc(ex_done, 1)

            def att_b(a):
                for i in range(2):
                    act.wait_ge(pT_done, 2 * a + i + 1)
                    A.activation(PT[i], ps[:, 2 + i, :], ACT.Copy).then_inc(pT_act, 1)

            def sgu_a(t):
                act.wait_ge(lnv_done, t + 1)
                A.activation(lsd[:, :], var[:, :], ACT.Sqrt).then_inc(lsd_done, 1)

            def mix(t):
                act.wait_ge(mT_done, 2 * t + 1)
                A.activation(hT[:, 0:4, :], four(0), ACT.Copy).then_inc(mT_act, 1)

            def query(p, b0):
                for b in (b0, b0 + 1):
                    act.wait_ge(w_used, Q_BLK[p] + b + 1)
                    if b >= 2:
                        act.wait_ge(qt_done, 4 * p + b - 1)
                    A.activation(qs[p][b % 2], ps[:, b % 2, :], ACT.Copy).then_inc(qs_act, 1)

            def scores(p):
                if p > 0:
                    act.wait_ge(idx_ok, 8 * p)
                for b in range(4):
                    act.wait_ge(s_done, 4 * p + b + 1)
                    A.activation(S[:, 2 * b:2 * b + 2, :], ps[:, b, :].rearrange("p (a s) -> p a s", a=2),
                                 ACT.Copy).then_inc(s_act, 1)

            def s5_setup():
                act.wait_ge(thr_ok, 1)
                A.activation(ab, th, ACT.Abs)
                A.activation(sn_, th, ACT.Sin)
                act.drain()
                A.activation(cs_, ab, ACT.Sin, bias=half_pi, scale=-1.0).then_inc(cs5_ok, 1)
                act.wait_ge(n_ok, 1)
                A.activation(sin_n, kf, ACT.Sin, scale=-TURN)
                A.activation(cos_n, kf, ACT.Abs)
                act.drain()
                A.activation(cos_n, cos_n, ACT.Sin, bias=half_pi, scale=-TURN).then_inc(csn_ok, 1)
                for b in range(4):
                    act.wait_ge(bT_done, b + 1)
                    A.activation(bT[:, 4 * b:4 * b + 4, :], four(b), ACT.Copy).then_inc(bT_act, 1)

            def turn_counts(ci):
                c = ci % KC
                for j in range(4):
                    A.activation(turns[:, j, :], time_row, ACT.Copy, scale=thp[:, 4 * c + j:4 * c + j + 1])
                act.drain()
                A.activation(whole, turns, ACT.Copy, bias=ROUND).then_inc(whole_ok, 1)

            def tables(ci):
                act.wait_ge(frac_ok, ci + 1)
                if ci >= 2:
                    act.wait_ge(d_ok, 4 * (ci - 1))
                A.activation(tab[ci % 2][:, 1, :, :], whole, ACT.Sin, scale=-TURN)
                A.activation(tab[ci % 2][:, 0, :, :], whole, ACT.Abs)
                act.drain()
                A.activation(tab[ci % 2][:, 0, :, :], tab[ci % 2][:, 0, :, :], ACT.Sin, bias=half_pi,
                             scale=-TURN).then_inc(tab_ok, 1)
                act.drain()

            def s5(t, c):
                ci = KC * t + c
                if c == 0:
                    act.wait_ge(hT_act, 5 + 2 * t)
                    turn_counts(ci)
                    tables(ci)
                    if t == 0:
                        act.wait_ge(ld_c, 16)
                        act.wait_ge(cz_zero, 2)
                if c + 1 < KC:
                    turn_counts(ci + 1)
                if ci >= 2:
                    act.wait_ge(yc_done, 2 * (ci - 1))
                for g in range(2):
                    half = slice(64 * g, 64 * g + 64)
                    for v, (r, sign) in enumerate(((0, 1.0), (0, -1.0), (1, -1.0))):
                        A.activation(cmat[ci % 2][half, :, v, 16 * g:16 * g + 16], c_raw[half, r, 4 * c:4 * c + 4, :],
                                     ACT.Copy, scale=sign).then_inc(cz_ok, 1)
                if c + 1 < KC:
                    tables(ci + 1)

            def s5_end(t):
                act.wait_ge(ye_ok, 2 * (t + 1))
                A.activation(h[:, t, :], h[:, t, :], ACT.Gelu_apprx_tanh).then_inc(g_ok, 1)
                act.wait_ge(gT_done, 2 * t + 1)
                A.activation(hT[:, 0:4, :], four(0), ACT.Copy).then_inc(gT_act, 1)

            def glu(t):
                for b in range(2):
                    act.wait_ge(bias_ok, 2 * t + b + 1)
                    g = gate[:, b * BANK:(b + 1) * BANK]
                    A.activation(g, g, ACT.Sigmoid).then_inc(sig_ok, 1)

            def gate_exp(n):
                act.wait_ge(cs_ok, n + 1)
                if n >= 2:
                    act.wait_ge(diag_ok, n - 1)
                A.activation(gexp[n % 2][:, :], cs[n % 2][:, :], ACT.Exp, bias=ncs[n % 2][:, :],
                             accum_out=gsum[n % 2][:, :]).then_inc(exp_ok, 1)

            def gelu(n):
                act.wait_ge(u_free, 16 * (n + 1) + RING)
                A.activation(gel[n % 2][:, :], dots[n % 2][:, :], ACT.Gelu_apprx_tanh).then_inc(gel_ok, 1)

            stage = dict(norm=norm, z=z, s5_angle=s5_angle, qk_turn=qk_turn, att_a=att_a, att_b=att_b, sgu_a=sgu_a, mix=mix,
                         query=query, scores=scores, s5_setup=s5_setup, s5=s5, s5_end=s5_end, glu=glu)

            def run(stages):
                for name, *args in stages:
                    if name in stage:
                        stage[name](*args)

            run(PRELUDE)
            gate_exp(0)
            for n in range(GROUPS):
                if n + 1 < GROUPS:
                    gate_exp(n + 1)
                gelu(n)
                run(WORK[n])
            run(LAST)

        @block.tensor
        def _(pe):
            PE = nc.tensor

            def wait_hT(m):
                pe.wait_ge(hT_act, m + 1)
                pe.wait_ge(hT_dve, m + 1)

            def turn(bank, src, done):
                for a in range(4):
                    ins = PE.transpose(ps[:, bank, a * P:(a + 1) * P], src[:, a * P:(a + 1) * P], ident)
                ins.then_inc(done, 1)

            def product(bank, lhs, rhs, done):
                for k in range(KC):
                    ins = PE.matmul(ps[:, bank, :], lhs[:, k, :], rhs[:, k, :], start=(k == 0), stop=(k == KC - 1))
                ins.then_inc(done, 1)

            def stream(bank, w):
                pe.wait_ge(ld_w[w % 2], 16 * (w // 2 + 1))
                product(bank, hT, wst[:, w % 2, :, :], w_used)

            def norm(m):
                if m < 8:
                    if m == 0:
                        pe.wait_ge(ld_cst, 16)
                    if m == 1:
                        wait_hT(0)
                    pe.wait_ge(h_done, m + 1)
                    if m == 4:
                        pe.wait_ge(bT_act, 4)
                    if m == 6:
                        pe.wait_ge(s_act, 12)
                    for b in range(2):
                        turn(b, h[:, NORM_T[m], b * BANK:(b + 1) * BANK], nT_done)

            def z(zi):
                t, n = Z_ORDER[zi]
                wait_hT(t)
                pe.wait_ge(ld_win[n], 16)
                if zi >= 2:
                    on_dve = Z_ORDER[zi - 2][1] < 2
                    pe.wait_ge(z_dve if on_dve else z_act, z_evacs(zi - 1, on_dve))
                product(4 + zi % 2, hT_of(t), win[n], z_done)

            def qk_turn(t):
                pe.wait_ge(z_dve, 2 * (t + 1))
                if t == 1:
                    pe.wait_ge(pT_act, 2)
                for w in range(2):
                    turn(2 + w, qk[w], qkT_done)

            def att_a(a):
                t, units = att_units(a)
                keys = P * (t + 1)
                pe.wait_ge(qT_act, t + 1)
                pe.wait_ge(kT_dve, t + 1)
                if a == 1:
                    pe.wait_ge(s_act, 4)
                for i, (h0, nh) in enumerate(units):
                    for j in range(nh):
                        hd = h0 + 2 * j
                        r = slice(HD * (hd % 2), HD * (hd % 2) + HD)
                        ins = PE.matmul(ps[:, i, j * keys:(j + 1) * keys], aqT[r, hd // 2, t * P:(t + 1) * P],
                                        akT[r, hd // 2, 0:keys], start=True, stop=True)
                    ins.then_inc(sc_done, 1)

            def att_b(a):
                t, units = att_units(a)
                for i in range(2):
                    pe.wait_ge(p_done, 2 * a + i + 1)
                    turn(2 + i, E[i], pT_done)
                for i, (h0, nh) in enumerate(units):
                    pe.wait_ge(pT_act, 2 * a + i + 1)
                    for j in range(nh):
                        hd = h0 + 2 * j
                        for kt in range(t + 1):
                            blk = j * (t + 1) + kt
                            ins = PE.matmul(ps[:, 6, hd * HD:(hd + 1) * HD], PT[i][:, blk * P:(blk + 1) * P],
                                            vv[:, kt, hd * HD:(hd + 1) * HD], start=(kt == 0), stop=(kt == t))
                ins.then_inc(o_done, 1)

            def sgu_b(t):
                pe.wait_ge(sgm_ok, 1)
                pe.wait_ge(g_done, t + 1)
                for g in range(8):
                    ins = PE.matmul(ps[:, 7, g * 64:(g + 1) * 64], sgw[:, g * P:(g + 1) * P], zg[:, t, g * 64:(g + 1) * 64],
                                    start=True, stop=True)
                ins.then_inc(sp_done, 1)

            def mix(t):
                pe.wait_ge(mix_done, t + 1)
                for b in range(2):
                    turn(b, h[:, t, b * BANK:(b + 1) * BANK], mT_done)

            def w_out_(t):
                pe.wait_ge(mT_act, t + 1)
                pe.wait_ge(mT_dve, t + 1)
                for b in range(2):
                    stream(2 + b, WOUT_BLK[t] + b)

            def query(p, b0):
                wait_hT(Q_NORM[p])
                for b in (b0, b0 + 1):
                    if b >= 2:
                        pe.wait_ge(qs_act, 4 * p + b - 1)
                    stream(b % 2, Q_BLK[p] + b)
                if p == 0 and b0 == 0:
                    pe.wait_ge(qT_act, 2)
                    pe.wait_ge(kT_dve, 2)
                for b in (b0, b0 + 1):
                    pe.wait_ge(qs_act, 4 * p + b + 1)
                    if b >= 2:
                        pe.wait_ge(qt_dve, 4 * p + b - 1)
                    turn(2 + b % 2, qs[p][b % 2], qt_done)

            def scores(p):
                pe.wait_ge(qt_dve, 4 * (p + 1))
                pe.wait_ge(ld_sk, 16)
                for b in range(4):
                    for a in range(4):
                        hp = 4 * b + a
                        ins = PE.matmul(ps[:, b, a * P:(a + 1) * P], qT[p][:, hp, :], sk[:, p // 2, hp % 2, :],
                                        start=True, stop=True)
                    ins.then_inc(s_done, 1)

            def s5_setup():
                pe.wait_ge(b_ok, 1)
                pe.wait_ge(s_act, 8)
                for b in range(4):
                    for a in range(4):
                        c, r = (4 * b + a) // 2, a % 2
                        ins = PE.transpose(ps[:, b, a * P:(a + 1) * P],
                                           bs[:, c, r, :, :, :].rearrange("p j g n -> p (j g n)"), ident)
                    ins.then_inc(bT_done, 1)

            def s5_in(t, pr):
                pi = 16 * t + pr
                if pi >= 2:
                    pe.wait_ge(w_ok, pi - 1)
                c = pr // 2
                for j in (2 * (pr % 2), 2 * (pr % 2) + 1):
                    rows = slice(32 * j, 32 * j + 32)
                    for r in range(2):
                        ins = PE.matmul(ps[:, j, r * P:(r + 1) * P], bT[rows, 2 * c + r, :], hT[rows, c, :],
                                        start=True, stop=True)
                ins.then_inc(xs_done, 1)

            def s5_out(t, pr):
                pi = 16 * t + pr
                c = pr // 2
                pe.wait_ge(d_ok, 2 * (pi + 1))
                pe.wait_ge(cz_ok, 6 * (KC * t + c + 1))
                by_cos, by_sin = prod[pi % 2]
                for i in range(2):
                    j = 2 * (pr % 2) + i
                    tile = 4 * c + j
                    o = ps[:, 4 + 2 * t + tile // 16, 32 * (tile % 16):32 * (tile % 16) + 32]
                    m = cmat[c % 2]
                    terms = ((by_cos[:, i, 0, :], 0), (by_sin[:, i, 1, :], 1), (by_sin[:, i, 0, :], 2), (by_cos[:, i, 1, :], 2))
                    for q, (d, v) in enumerate(terms):
                        ins = PE.matmul(o, d, m[:, j, v, :], start=(q == 0), stop=(q == 3))
                ins.then_inc(yc_done, 1)

            def s5(t, c):
                if c == 0:
                    wait_hT(4 + 2 * t)
                    pe.wait_ge(bT_act, 4)
                    s5_in(t, 0)
                for pr in (2 * c, 2 * c + 1):
                    if pr + 1 < 16:
                        s5_in(t, pr + 1)
                    s5_out(t, pr)

            def s5_end(t):
                pe.wait_ge(g_ok, t + 1)
                for b in range(2):
                    turn(b, h[:, t, b * BANK:(b + 1) * BANK], gT_done)

            def glu(t):
                pe.wait_ge(gT_act, t + 1)
                pe.wait_ge(gT_dve, t + 1)
                for b in range(2):
                    stream(2 + b, GLU_BLK[t] + b)

            def experts(n):
                t = n // PH % T
                pe.wait_ge(diag_ok, n + 1)
                for s in range(TOPK):
                    pe.wait_ge(got_v[s % RING], 16 * (2 * n + 1 + s // RING))
                    for b in range(2):
                        ins = PE.matmul(ps[:, 4 + 2 * t + b, :], diag[n % 2][:, s, :], ringv[:, s % RING, b * BANK:(b + 1) * BANK],
                                        start=(n % PH == 0 and s == 0), stop=(n % PH == PH - 1 and s == TOPK - 1))
                    ins.then_inc(v_free, 1)

            stage = dict(norm=norm, z=z, qk_turn=qk_turn, att_a=att_a, att_b=att_b, sgu_b=sgu_b, mix=mix, w_out=w_out_,
                         query=query, scores=scores, s5_setup=s5_setup, s5=s5, s5_end=s5_end, glu=glu)

            def run(stages):
                for name, *args in stages:
                    if name in stage:
                        stage[name](*args)

            run(PRELUDE)
            for n in range(GROUPS):
                if n > 0:
                    experts(n - 1)
                run(WORK[n])
            experts(GROUPS - 1)

        @block.vector
        def _(dve):
            V = nc.vector

            def norm(m):
                t = NORM_T[m]
                dve.wait_ge(sq_done, m + 1)
                V.tensor_scalar(ms[:, t:t + 1], ss[:, t:t + 1], 1.0 / D, RMS_EPS, ALU.mult, ALU.add).then_inc(ms_done, 1)
                dve.wait_ge(sd_done, m + 1)
                V.reciprocal(rstd[:, t:t + 1], sd[:, t:t + 1])
                dve.drain()
                v = NORM_VEC[m]
                dve.wait_ge(ld_vec[v % 2], 16 * (v // 2 + 1))
                V.scalar_tensor_tensor(h[:, t, :], x[:, t, :], rstd[:, t:t + 1], vec[:, v % 2, :], ALU.mult,
                                       ALU.mult).then_inc(h_done, 1)
                if m < 8:
                    dve.wait_ge(nT_done, 2 * m + 2)
                    V.tensor_copy(hT_of(m)[:, 4:8, :], four(1)).then_inc(hT_dve, 1)

            def residual(t, b, term):
                xs = x[:, t, b * BANK:(b + 1) * BANK]
                V.tensor_tensor(xs, xs, term, ALU.add).then_inc(x_done, 1)

            def z(zi):
                t, w = Z_ORDER[zi]
                if w >= 2:
                    return
                dve.wait_ge(z_done, zi + 1)
                z4 = ps[:, 4 + zi % 2, :].rearrange("p (h a d) -> p h a d", h=HEADS, a=2)
                a4 = rot_a.rearrange("p (h a d) -> p h a d", h=HEADS, a=2)
                b4 = rot_b.rearrange("p (h a d) -> p h a d", h=HEADS, a=2)
                V.tensor_tensor(a4, z4, bc(cos_t[:, t, :], [HEADS, 2, None]), ALU.mult)
                V.tensor_tensor(b4[:, :, 0, :], z4[:, :, 1, :], bc(nsin_t[:, t, :], [HEADS, None]), ALU.mult)
                V.tensor_tensor(b4[:, :, 1, :], z4[:, :, 0, :], bc(sin_t[:, t, :], [HEADS, None]), ALU.mult)
                dve.drain()
                if t == 1:
                    dve.wait_ge(qkT_done, 2)
                V.tensor_tensor(qk[w], rot_a, rot_b, ALU.add).then_inc(z_dve, 1)
                dve.drain()

            def s5_angle():
                dve.wait_ge(dt_ok, 1)
                V.tensor_tensor(th, lam_i, dt_, ALU.mult)
                V.tensor_tensor(lrdt, lam_r, dt_, ALU.mult).then_inc(th_ok, 1)
                dve.drain()
                V.tensor_scalar(kf, th, INV_TWO_PI, ROUND, ALU.mult, ALU.add)
                dve.drain()
                V.tensor_scalar(kf, kf, ROUND, None, ALU.subtract)
                dve.drain()
                V.scalar_tensor_tensor(th, kf, -TWO_PI_HI, th, ALU.mult, ALU.add)
                dve.drain()
                V.scalar_tensor_tensor(th, kf, -TWO_PI_LO, th, ALU.mult, ALU.add)
                dve.drain()
                V.tensor_scalar(th, th, PI_BELOW, -PI_BELOW, ALU.min, ALU.max).then_inc(thr_ok, 1)
                dve.drain()
                V.tensor_scalar(thp, th, INV_TWO_PI, None, ALU.mult)
                dve.drain()

            def qk_turn(t):
                dve.wait_ge(qkT_done, 2 * t + 2)
                V.tensor_copy(akT[:, :, t * P:(t + 1) * P], four(3)).then_inc(kT_dve, 1)

            def att_a(a):
                t, units = att_units(a)
                for i, (h0, nh) in enumerate(units):
                    cols = slice(8 * t + h0, 8 * t + h0 + 2 * nh - 1, 2)
                    dve.wait_ge(sc_done, 2 * a + i + 1)
                    e3 = E[i].rearrange("p (h k) -> p h k", h=nh)
                    V.scalar_tensor_tensor(e3, ps[:, i, :].rearrange("p (h k) -> p h k", h=nh), SCALE,
                                           bc(negm[t], [nh, None]), ALU.mult, ALU.add)
                    dve.drain()
                    V.tensor_reduce(negmax[:, cols], e3, AX.X, ALU.max, negate=True).then_inc(nm_done, 1)
                for i, (h0, nh) in enumerate(units):
                    cols = slice(8 * t + h0, 8 * t + h0 + 2 * nh - 1, 2)
                    dve.wait_ge(ex_done, 2 * a + i + 1)
                    e3 = E[i].rearrange("p (h k) -> p h k", h=nh)
                    V.tensor_tensor(e3, e3, bc(count[t], [nh, None]), ALU.mult)
                    dve.drain()
                    V.tensor_reduce(den[:, cols], e3, AX.X, ALU.add).then_inc(p_done, 1)

            def sgu_a(t):
                dve.wait_ge(z_act, 2 + 3 * t)
                g3 = zg[:, t, :].rearrange("p (g d) -> p g d", g=8)
                s3 = sg_tmp.rearrange("p (g d) -> p g d", g=8)
                V.tensor_reduce(mu[:, :], g3, AX.X, ALU.add)
                dve.drain()
                V.scalar_tensor_tensor(g3, bc(mu[:, :], [None, 64]), -1.0 / 64, g3, ALU.mult, ALU.add)
                dve.drain()
                V.tensor_tensor(s3, g3, g3, ALU.mult)
                dve.drain()
                V.tensor_reduce(var[:, :], s3, AX.X, ALU.add)
                dve.drain()
                V.tensor_scalar(var[:, :], var[:, :], 1.0 / 64, LN_EPS, ALU.mult, ALU.add).then_inc(lnv_done, 1)
                dve.wait_ge(lsd_done, t + 1)
                V.reciprocal(lrs[:, :], lsd[:, :])
                dve.drain()
                V.tensor_tensor(g3, g3, bc(lrs[:, :], [None, 64]), ALU.mult)
                dve.drain()
                dve.wait_ge(ld_sgu, 48)
                V.tensor_tensor(zg[:, t, :], zg[:, t, :], sg_gain, ALU.mult).then_inc(g_done, 1)

            def sgu_b(t):
                dve.wait_ge(sp_done, t + 1)
                dve.wait_ge(z_act, 3 + 3 * t)
                s3 = sg_tmp.rearrange("p (g d) -> p g d", g=8)
                V.tensor_tensor(s3, ps[:, 7, :].rearrange("p (g d) -> p g d", g=8), bc(sgb[:, :], [None, 64]), ALU.add)
                dve.drain()
                V.tensor_tensor(h[:, t, AW:2 * AW], sg_tmp, zu[:, t, :], ALU.mult)
                dve.drain()

            def mix(t):
                dve.wait_ge(o_done, (1, 3)[t])
                V.reciprocal(rden[:, 8 * t:8 * t + 8], den[:, 8 * t:8 * t + 8])
                dve.drain()
                V.tensor_tensor(h[:, t, 0:AW].rearrange("p (h d) -> p h d", h=HEADS),
                                ps[:, 6, :].rearrange("p (h d) -> p h d", h=HEADS),
                                bc(rden[:, 8 * t:8 * t + 8], [None, HD]), ALU.mult).then_inc(mix_done, 1)
                dve.wait_ge(mT_done, 2 * t + 2)
                V.tensor_copy(hT[:, 4:8, :], four(1)).then_inc(mT_dve, 1)

            def w_out_(t):
                for b in range(2):
                    dve.wait_ge(w_used, WOUT_BLK[t] + b + 1)
                    residual(t, b, ps[:, 2 + b, :])

            def query(p, b0):
                for b in (b0, b0 + 1):
                    dve.wait_ge(qt_done, 4 * p + b + 1)
                    V.tensor_copy(qT[p][:, 4 * b:4 * b + 4, :], four(2 + b % 2)).then_inc(qt_dve, 1)

            def y_sum(r):
                t = (0, 1, 0, 1)[(2, 4, 6, 7).index(r)]
                phase = (2, 4, 6, 7).index(r)
                dve.wait_ge(v_free, RING + 16 * PH * (phase + 1))
                for b in range(2):
                    residual(t, b, ps[:, 4 + 2 * t + b, :])

            def s5_setup():
                V.memset(bs, 0.0)
                V.memset(cmat[0], 0.0).then_inc(cz_zero, 1)
                V.memset(cmat[1], 0.0).then_inc(cz_zero, 1)
                V.tensor_scalar(mag, thp, float(P), None, ALU.mult)
                dve.drain()
                V.tensor_scalar(kf, mag, ROUND, None, ALU.add)
                dve.drain()
                V.scalar_tensor_tensor(kf, kf, ROUND, mag, ALU.subtract, ALU.subtract).then_inc(n_ok, 1)
                dve.wait_ge(cs5_ok, 1)
                dve.wait_ge(dec_ok, 1)
                dve.drain()
                V.tensor_tensor(ar, dec, cs_, ALU.mult)
                V.tensor_tensor(ai, dec, sn_, ALU.mult)
                V.tensor_tensor(mag, lam_r, lam_r, ALU.mult)
                V.tensor_tensor(lrdt, lam_i, lam_i, ALU.mult)
                dve.drain()
                V.tensor_tensor(mag, mag, lrdt, ALU.add)
                V.tensor_scalar(ar, ar, 1.0, None, ALU.subtract)
                dve.drain()
                V.reciprocal(mag, mag)
                V.tensor_tensor(kr, ar, lam_r, ALU.mult)
                V.tensor_tensor(lrdt, ai, lam_i, ALU.mult)
                V.tensor_tensor(ki, ai, lam_r, ALU.mult)
                V.tensor_tensor(ab, ar, lam_i, ALU.mult)
                dve.drain()
                V.tensor_tensor(kr, kr, lrdt, ALU.add)
                V.tensor_tensor(ki, ki, ab, ALU.subtract)
                dve.drain()
                V.tensor_tensor(kr, kr, mag, ALU.mult)
                V.tensor_tensor(ki, ki, mag, ALU.mult)
                dve.drain()
                dve.wait_ge(ld_b, 16)
                for r in range(2):
                    for dst, k_, r_ in ((bt1, kr, r), (bt2, ki, 1 - r)):
                        V.tensor_tensor(dst.rearrange("p (i n) -> p i n", i=S5_TILES), bc(k_, [None, 16]),
                                        b_raw[:, r_, :].rearrange("p (i n) -> p i n", i=S5_TILES), ALU.mult)
                    dve.drain()
                    for g in range(2):
                        half = slice(64 * g, 64 * g + 64)
                        ins = V.tensor_tensor(bs[half, :, r, :, g, :],
                                              bt1[half, :].rearrange("p (c j n) -> p c j n", c=8, j=4),
                                              bt2[half, :].rearrange("p (c j n) -> p c j n", c=8, j=4),
                                              (ALU.subtract, ALU.add)[r])
                    if r == 0:
                        dve.drain()
                ins.then_inc(b_ok, 1)

            def fraction(ci):
                dve.wait_ge(whole_ok, ci + 1)
                V.scalar_tensor_tensor(whole, whole, ROUND, turns, ALU.subtract, ALU.subtract).then_inc(frac_ok, 1)

            def s5_pair(t, pr):
                pi, c = 16 * t + pr, pr // 2
                js = slice(2 * (pr % 2), 2 * (pr % 2) + 2)
                cos, sin = (bc_pair(tab[c % 2][:, r, js, :]) for r in range(2))
                by_cos, by_sin = prod[pi % 2]
                dve.wait_ge(xs_done, pi + 1)
                dve.wait_ge(tab_ok, KC * t + c + 1)
                if pi >= 2:
                    dve.wait_ge(yc_done, pi - 1)
                x4 = ps[:, js, 0:2 * P].rearrange("p i (r s) -> p i r s", r=2)
                V.tensor_tensor(by_cos, x4, cos, ALU.mult)
                V.tensor_tensor(by_sin, x4, sin, ALU.mult)
                dve.drain()
                V.tensor_tensor(by_cos[:, :, 0, :], by_cos[:, :, 0, :], by_sin[:, :, 1, :], ALU.add)
                V.tensor_tensor(by_cos[:, :, 1, :], by_cos[:, :, 1, :], by_sin[:, :, 0, :], ALU.subtract).then_inc(w_ok, 1)
                dve.drain()
                for i in range(2):
                    tile = 4 * c + js.start + i
                    for r in range(2):
                        V.tensor_tensor_scan(zst[:, i, r, :], dec[:, tile:tile + 1].to_broadcast([P, P]), by_cos[:, i, r, :],
                                             z_init[:, r, tile:tile + 1] if t else 0.0, ALU.mult, ALU.add)
                dve.drain()
                V.tensor_tensor(by_cos, zst, cos, ALU.mult).then_inc(d_ok, 1)
                V.tensor_tensor(by_sin, zst, sin, ALU.mult).then_inc(d_ok, 1)
                if t == 0:
                    tile = 4 * c + js.start
                    V.tensor_copy(z_last[:, tile:tile + 2, :], zst[:, :, :, P - 1])
                dve.drain()

            def bc_pair(ap):
                return ap.unsqueeze(2).to_broadcast([P, 2, 2, P])

            def s5(t, c):
                ci = KC * t + c
                if c == 0:
                    fraction(ci)
                    if t == 1:
                        dve.wait_ge(csn_ok, 1)
                        zr, zi = z_last[:, :, 0], z_last[:, :, 1]
                        V.tensor_tensor(kr, cos_n, zr, ALU.mult)
                        V.tensor_tensor(ki, sin_n, zi, ALU.mult)
                        V.tensor_tensor(ar, sin_n, zr, ALU.mult)
                        V.tensor_tensor(ai, cos_n, zi, ALU.mult)
                        dve.drain()
                        V.tensor_tensor(z_init[:, 0, :], kr, ki, ALU.subtract)
                        V.tensor_tensor(z_init[:, 1, :], ar, ai, ALU.add)
                s5_pair(t, 2 * c)
                if c + 1 < KC:
                    fraction(ci + 1)
                s5_pair(t, 2 * c + 1)

            def s5_end(t):
                v = D_VEC[t]
                dve.wait_ge(ld_vec[v % 2], 16 * (v // 2 + 1))
                V.tensor_tensor(h[:, t, :], h[:, t, :], vec[:, v % 2, :], ALU.mult).then_inc(dh_done, 1)
                dve.drain()
                dve.wait_ge(yc_done, 16 * (t + 1))
                for b in range(2):
                    hs = h[:, t, b * BANK:(b + 1) * BANK]
                    V.tensor_tensor(hs, hs, ps[:, 4 + 2 * t + b, :], ALU.add).then_inc(ye_ok, 1)
                dve.wait_ge(gT_done, 2 * t + 2)
                V.tensor_copy(hT[:, 4:8, :], four(1)).then_inc(gT_dve, 1)

            def glu(t):
                v = BIAS_VEC[t]
                dve.wait_ge(ld_vec[v % 2], 16 * (v // 2 + 1))
                for b in range(2):
                    cols = slice(b * BANK, (b + 1) * BANK)
                    dve.wait_ge(w_used, GLU_BLK[t] + b + 1)
                    V.tensor_tensor(gate[:, cols], ps[:, 2 + b, :], vec[:, v % 2, cols], ALU.add).then_inc(bias_ok, 1)
                for b in range(2):
                    cols = slice(b * BANK, (b + 1) * BANK)
                    dve.wait_ge(sig_ok, 2 * t + b + 1)
                    V.tensor_tensor(gate[:, cols], gate[:, cols], h[:, t, cols], ALU.mult)
                    dve.drain()
                    residual(t, b, gate[:, cols])

            def route(n):
                keys = S[:, n % PH, :].rearrange("p (a k) -> p a k", a=2)
                top_cs = cs[n % 2]
                dve.wait_ge(s_act, 4 * (n // PH + 1))
                for p in range(2):
                    V.max(top[:, p, 0:8], keys[:, p, :])
                dve.drain()
                for p in range(2):
                    V.max_index(top_i[:, p, 0:8], top[:, p, 0:8], keys[:, p, :])
                    V.match_replace(key_b[:, p, :], top[:, p, 0:8], keys[:, p, :], LOWEST)
                dve.drain()
                for p in range(2):
                    V.max(top[:, p, 8:16], key_b[:, p, :])
                dve.drain()
                for p in range(2):
                    V.max_index(top_i[:, p, 8:16], top[:, p, 8:16], key_b[:, p, :])
                V.tensor_tensor(cand_a[:, :].rearrange("p (a b) -> p a b", a=TOPK), bc(top[:, 0, :], [None, TOPK]),
                                bc(top[:, 1, :], [TOPK, None]), ALU.add)
                dve.drain()
                V.max(top_cs[:, 0:8], cand_a[:, :])
                V.tensor_scalar(top_f[:, 0, :], top_i[:, 0, :], float(NK * (n // (T * PH))), None, ALU.add)
                V.tensor_copy(top_f[:, 1, :], top_i[:, 1, :])
                dve.drain()
                V.max_index(pos_i[:, 0:8], top_cs[:, 0:8], cand_a[:, :])
                V.match_replace(cand_b[:, :], top_cs[:, 0:8], cand_a[:, :], LOWEST)
                V.tensor_scalar(ncs[n % 2][:, :], top_cs[:, 0:1], -1.0, None, ALU.mult)
                dve.drain()
                V.max(top_cs[:, 8:16], cand_b[:, :])
                dve.drain()
                V.max_index(pos_i[:, 8:16], top_cs[:, 8:16], cand_b[:, :]).then_inc(cs_ok, 1)
                dve.drain()
                V.tensor_scalar(pos_ab[:, 0, :], pos_i[:, :], 4, None, ALU.logical_shift_right)
                V.tensor_scalar(pos_ab[:, 1, :], pos_i[:, :], 15, None, ALU.bitwise_and)
                dve.drain()
                hot = [c[:, :].rearrange("p (a b) -> p a b", a=TOPK) for c in (cand_a, cand_b)]
                for p in range(2):
                    V.tensor_tensor(hot[p], bc(pos_ab[:, p, :], [None, TOPK]), bc(iota16, [TOPK, None]), ALU.is_equal)
                dve.drain()
                for p in range(2):
                    V.tensor_tensor(hot[p], hot[p], bc(top_f[:, p, :], [TOPK, None]), ALU.mult)
                dve.drain()
                for p in range(2):
                    V.tensor_reduce(row[:, p, :], hot[p], AX.X, ALU.add)
                dve.drain()
                if n >= 4:
                    dve.wait_ge(v_free, 16 * (n - 3) + RING)
                V.scalar_tensor_tensor(idx[n % 4][:, :], row[:, 0, :], float(NK), row[:, 1, :], ALU.mult,
                                       ALU.add).then_inc(idx_ok, 1)

            def dot_products(n):
                t = n // PH % T
                for s in range(TOPK):
                    u = ringu[:, s % RING, :]
                    dve.wait_ge(got_u[s % RING], 16 * (2 * n + 1 + s // RING))
                    V.tensor_tensor_reduce(out=u, in0=u, in1=h[:, t, :], scale=1.0, scalar=0.0, op0=ALU.mult, op1=ALU.add,
                                           accum_out=dots[n % 2][:, s:s + 1]).then_inc(u_free, 1)

            def weights(n):
                i = n % 2
                dve.wait_ge(exp_ok, n + 1)
                V.reciprocal(grec[i][:, :], gsum[i][:, :])
                dve.drain()
                dve.wait_ge(gel_ok, n + 1)
                V.scalar_tensor_tensor(wgt[i][:, :], gexp[i][:, :], grec[i][:, :], gel[i][:, :], ALU.mult, ALU.mult)
                dve.drain()
                if n >= 2:
                    dve.wait_ge(v_free, 16 * (n - 1) + RING)
                V.tensor_tensor(diag[i], bc(ident, [TOPK, None]), bc(wgt[i][:, :], [None, P]), ALU.mult).then_inc(diag_ok, 1)

            stage = dict(norm=norm, z=z, s5_angle=s5_angle, qk_turn=qk_turn, att_a=att_a, att_b=None, sgu_a=sgu_a, sgu_b=sgu_b,
                         mix=mix, w_out=w_out_, query=query, y_sum=y_sum, s5_setup=s5_setup, s5=s5, s5_end=s5_end, glu=glu)

            def run(stages):
                for name, *args in stages:
                    if stage.get(name):
                        stage[name](*args)

            V.memset(rden[:, 0:1], 0.0).then_inc(u_free, RING)
            V.memset(rden[:, 1:2], 0.0).then_inc(v_free, RING)
            run(PRELUDE)
            route(0)
            for n in range(GROUPS):
                if n + 1 < GROUPS:
                    route(n + 1)
                dot_products(n)
                run(WORK[n])
                weights(n)
            run(LAST)


def constants():
    import numpy as np
    c = np.zeros((P, C_ALL), np.float32)
    c[:, C_ID:C_ID + P] = np.eye(P, dtype=np.float32)
    tok = np.arange(SEQ)
    d = tok[:, None] - tok[None, :]
    cnt = ((d >= 0) & (d <= 128)).astype(np.float32)
    for window, dil in ((512, 4), (2048, 16)):
        cnt += ((d >= 0) & (d <= window) & (d % dil == 0)).astype(np.float32)
    neg = np.where(cnt > 0, np.float32(0), np.float32(-1e37))
    half = HD // 2
    inv = np.power(np.float32(10000.0), (-2.0 * np.arange(half, dtype=np.float32) / HD).astype(np.float32))
    ang = tok.astype(np.float32)[:, None] * inv.astype(np.float32)[None, :]
    for t in range(T):
        r = slice(t * P, (t + 1) * P)
        keys = P * (t + 1)
        c[:, C_CNT + P * t:C_CNT + P * t + keys] = cnt[r, :keys]
        c[:, C_NEG + P * t:C_NEG + P * t + keys] = neg[r, :keys]
        c[:, C_COS + half * t:C_COS + half * (t + 1)] = np.cos(ang[r])
        c[:, C_SIN + half * t:C_SIN + half * (t + 1)] = np.sin(ang[r])
        c[:, C_NSIN + half * t:C_NSIN + half * (t + 1)] = -np.sin(ang[r])
    c[:, C_IOTA:C_IOTA + 16] = np.arange(16)
    c[:, C_TIME:C_TIME + P] = np.arange(P)
    c[:, C_HPI] = np.pi / 2
    return c


def kernel(x, norm_mix_g, norm_ffn_g, final_norm_g, mix_w_in, sgu_norm_g, sgu_w, sgu_b, mix_w_out, s5_lambda_re,
           s5_lambda_im, s5_b_re, s5_b_im, s5_c_re, s5_c_im, s5_d, s5_log_step, glu_w, glu_b, peer_wq, peer_subkeys,
           peer_u, peer_v):
    import numpy as np
    import concourse.bacc as bacc
    from concourse.bass_utils import run_bass_kernel_spmd as run

    a = np.asarray

    def states(v):
        v = a(v)
        v = v.reshape((32, 2, 64) + v.shape[2:])
        return v.transpose((1, 2, 0) + tuple(range(3, v.ndim))).reshape((P, 32) + v.shape[3:])

    log_step = np.broadcast_to(a(s5_log_step)[0][:, None], (64, 64))
    data = {
        "x": a(x).reshape(SEQ, D),
        "vecs": np.stack([a(norm_mix_g)[0], a(norm_ffn_g)[0], a(norm_mix_g)[1], a(norm_ffn_g)[1], a(final_norm_g),
                          a(s5_d)[0], a(glu_b)[0]]),
        "cst": constants(),
        "w_in": a(mix_w_in)[0],
        "sgu_g": a(sgu_norm_g)[0].reshape(1, AW),
        "sgu_wT": a(sgu_w)[0].transpose(2, 0, 1).reshape(P, 8 * P),
        "sgu_bT": a(sgu_b)[0].T,
        "w_out": a(mix_w_out)[0],
        "s5_par": np.concatenate([states(a(s5_lambda_re)[0]), states(a(s5_lambda_im)[0]), states(log_step)], axis=1),
        "s5_b": np.stack([states(a(s5_b_re)[0]).reshape(P, 512), states(a(s5_b_im)[0]).reshape(P, 512)], axis=1),
        "s5_c": np.stack([states(a(s5_c_re)[0].transpose(0, 2, 1)), states(a(s5_c_im)[0].transpose(0, 2, 1))], axis=1),
        "glu_w": a(glu_w)[0],
        "wq": a(peer_wq),
        "skT": a(peer_subkeys).transpose(3, 0, 1, 2),
        "u_tab": a(peer_u).reshape(2 * EXPERTS, D),
        "v_tab": a(peer_v).reshape(2 * EXPERTS, D),
    }
    nc = bacc.Bacc("TRN2", target_bir_lowering=False, num_devices=1)
    arrays, args = {}, []
    for name, v in data.items():
        v = np.ascontiguousarray(v)
        arrays[f"in_{name}_dram"] = v
        args.append(nc.dram_tensor(f"in_{name}_dram", v.shape, mybir.dt.from_np(v.dtype), kind="ExternalInput").ap())
    args.append(nc.dram_tensor("out_0_dram", (SEQ, D), F32, kind="ExternalOutput").ap())
    trunk(nc, *args)
    r = run(nc, [arrays], core_ids=[0])
    return r.results[0]["out_0_dram"].reshape(1, SEQ, D)
```

```python
import math
from contextlib import ExitStack

import concourse.bass as bass
from concourse import mybir

ALU = mybir.AluOpType
ACT = mybir.ActivationFunctionType
AX = mybir.AxisListType
F32 = mybir.dt.float32
U32 = mybir.dt.uint32

P = 128
SEQ = 256
D = 1024
T = SEQ // P
KC = D // P
HEADS, HD = 8, 64
AW = HEADS * HD
BANK = 512
PH, NK, TOPK = 8, 128, 16
EXPERTS = NK * NK
GROUPS = 2 * T * PH
RING = 8
ROUTE_AT = 8
S5_TILES = 32
RMS_EPS, LN_EPS = 1e-6, 1e-5
SCALE = HD ** -0.5
LOWEST = -3.0e38
ROUND = 12582912.0
TWO_PI_HI = 6.28125
TWO_PI_LO = 2 * math.pi - 6.28125
INV_TWO_PI = 1 / (2 * math.pi)
TURN = 6.2831845
PI_BELOW = 3.1415925

NORM_T = [0, 1, 0, 1, 0, 0, 1, 1, 0, 1]
NORM_VEC = [0, 0, 1, 1, 2, 5, 6, 9, 10, 10]
VEC_ROW = [0, 1, 2, 5, 6, 3, 2, 5, 6, 3, 4]
D_VEC, BIAS_VEC = [3, 7], [4, 8]
WOUT_BLK = [0, 6]
GLU_BLK = [12, 18]
Q_BLK = [2, 8, 14, 20]
Q_NORM = [2, 3, 5, 7]
Z_ORDER = [(0, 0), (0, 1), (0, 2), (0, 4), (0, 3), (1, 0), (1, 1), (1, 2), (1, 4), (1, 3)]

PRELUDE = [("norm", 0), ("norm_T", 0), ("z", 0), ("z", 1), ("z", 2), ("qk_turn", 0), ("att_a", 0), ("norm", 1), ("z", 3),
           ("z", 4), ("sgu_a", 0), ("att_b", 0), ("norm_T", 1), ("sgu_b", 0), ("mix", 0), ("mix_T", 0), ("w_out", 0, 0),
           ("w_out", 0, 1), ("norm", 2), ("norm_T", 2), ("q_in", 0, 0), ("q_turn", 0, 0), ("q_score", 0, 0)]


def between():
    work = {n: {} for n in range(GROUPS)}

    def at(n, slot, *stages):
        work[n].setdefault(slot, []).extend(stages)

    def query(n, slot, phase, b):
        for i, name in enumerate(("q_in", "q_turn", "q_score")):
            at(n, slot + i, (name, phase, b))

    at(0, 0, ("z", 5), ("z", 6), ("z", 7), ("qk_turn", 1), ("z", 8), ("z", 9))
    query(0, 12, 0, 1)
    at(1, 1, ("sgu_a", 1))
    at(1, 4, ("att_a", 1))
    at(1, 6, ("att_b", 1))
    query(1, 10, 0, 2)
    at(2, 2, ("att_a", 2))
    at(2, 4, ("att_b", 2))
    at(2, 6, ("sgu_b", 1))
    query(2, 10, 0, 3)
    at(3, 1, ("mix", 1))
    at(3, 3, ("mix_T", 1))
    at(3, 4, ("w_out", 1, 0))
    at(3, 11, ("w_out", 1, 1))
    at(4, 1, ("norm", 3))
    at(4, 4, ("norm_T", 3))
    query(4, 8, 1, 0)
    at(5, 2, ("s5_angle",))
    query(5, 8, 1, 1)
    at(6, 2, ("s5_setup",))
    query(6, 10, 1, 2)
    query(7, 4, 1, 3)
    for t in range(T):
        g = PH * (t + 1)
        at(g + 1, 0, ("y_sum", 2 + 2 * t), ("norm", 4 + 2 * t))
        at(g + 1, 3, ("norm_T", 4 + 2 * t))
        for pair in range(S5_TILES // 2):
            slot = 20 + 22 * pair // 5
            at(g + slot // TOPK, slot % TOPK, ("s5", t, pair))
        at(g + 5, 9, ("s5_end", t))
        at(g + 5, 11, ("gate_T", t))
        at(g + 5, 12, ("glu", t, 0))
        at(g + 6, 5, ("glu", t, 1))
        at(g + 6, 12, ("norm", 5 + 2 * t))
        at(g + 6, 15, ("norm_T", 5 + 2 * t))
        query(g + 7, 0, 2 + t, 0)
        query(g + 7, 10, 2 + t, 1)
        query(g + 8, 3, 2 + t, 2)
        query(g + 8, 11, 2 + t, 3)
    at(25, 2, ("y_sum", 6), ("norm", 8))
    return work


WORK = between()
LAST = [("y_sum", 7), ("norm", 9)]

C_ID, C_CNT, C_NEG, C_COS, C_SIN, C_NSIN, C_IOTA, C_TIME, C_HPI = 0, 128, 512, 896, 960, 1024, 1088, 1104, 1232
C_ALL = 1233


def trunk(nc, x_in, vecs, cst_in, w_in, sgu_g, sgu_wT, sgu_bT, w_out, s5_par, s5_b, s5_c, glu_w, wq, skT, u_tab, v_tab,
          out):
    with ExitStack() as ctx:
        def sb(name, shape, dt=F32):
            return ctx.enter_context(nc.sbuf_tensor(name, shape, dt))

        def sem(name):
            return ctx.enter_context(nc.semaphore(name))

        x = sb("x", [P, T, D])
        h = sb("h", [P, T, D])
        hTs = [sb(f"hT{t}", [P, KC, P]) for t in range(T)]
        cst = sb("cst", [P, C_ALL])
        vec = sb("vec", [P, 2, D])
        sk = sb("sk", [P, 2, 2, NK])
        ss, ms, sd, rstd = (sb(n, [P, T]) for n in ("ss", "ms", "sd", "rstd"))
        rings = sb("rings", [P, 2 * RING * D])
        wst = sb("wst", [P, 2, KC, BANK])
        mem = sb("mem", [P, 9472])
        dgs = sb("dgs", [P, 2 * TOPK * P])
        scr = sb("scr", [P, 2048])
        sgw = sb("sgw", [P, D])
        ps = ctx.enter_context(nc.psum_tensor("ps", [P, 8, BANK], F32))

        def four(bank):
            return ps[:, bank, :].rearrange("p (a s) -> p a s", a=4)

        ident = cst[:, C_ID:C_ID + P]
        count = [cst[:, C_CNT + P * t:C_CNT + P * (2 * t + 1)] for t in range(T)]
        negm = [cst[:, C_NEG + P * t:C_NEG + P * (2 * t + 1)] for t in range(T)]
        cos_t = cst[:, C_COS:C_COS + 64].rearrange("p (t k) -> p t k", t=T)
        sin_t = cst[:, C_SIN:C_SIN + 64].rearrange("p (t k) -> p t k", t=T)
        nsin_t = cst[:, C_NSIN:C_NSIN + 64].rearrange("p (t k) -> p t k", t=T)
        iota16 = cst[:, C_IOTA:C_IOTA + 16]
        time_row = cst[:, C_TIME:C_TIME + P]
        half_pi = cst[:, C_HPI:C_HPI + 1]

        win = [rings[:, 4096 * i:4096 * (i + 1)] for i in range(3)] + [dgs[:, :], rings[:, 12288:16384]]
        win = [w.rearrange("p (k n) -> p k n", k=KC) for w in win]
        qk = [scr[:, 1024 + BANK * w:1536 + BANK * w] for w in range(2)]

        def part(start, size, pattern="p (a s) -> p a s", **dims):
            ap = mem[:, start:start + size]
            return ap.rearrange(pattern, **dims) if dims else ap

        akT, aqT = part(0, 1024, a=4), part(1024, 1024, a=4)
        vv, zu, zg = (part(2048 + 1024 * i, 1024, a=T) for i in range(3))
        E = [part(5120 + BANK * i, BANK) for i in range(2)]
        PT = [part(6144 + BANK * i, BANK) for i in range(2)]
        sg_tmp, sg_gain = (part(7168 + BANK * i, BANK) for i in range(2))
        rot_a, rot_b = (part(8448 + BANK * i, BANK) for i in range(2))
        negmax, den, rden = (sb(n, [P, 16]) for n in ("negmax", "den", "rden"))
        mu, var, lsd, lrs = (sb(n, [P, 8]) for n in ("mu", "var", "lsd", "lrs"))
        sgb = sb("sgb", [P, 8])

        ringu = rings[:, 0:RING * D].rearrange("p (b n) -> p b n", b=RING)
        ringv = rings[:, RING * D:].rearrange("p (b n) -> p b n", b=RING)
        qs = part(8448, BANK)
        qT = part(8960, BANK, a=4)
        S = scr[:, :].rearrange("p (g k) -> p g k", g=PH)
        diag = [dgs[:, 2048 * i:2048 * (i + 1)].rearrange("p (s t) -> p s t", s=TOPK) for i in range(2)]
        cand_a, cand_b = sb("cand_a", [P, 256]), sb("cand_b", [P, 256])
        key_b = cand_b[:, :].rearrange("p (a k) -> p a k", a=2)
        top = sb("top", [P, 2, TOPK])
        top_i = sb("top_i", [P, 2, TOPK], U32)
        top_f = sb("top_f", [P, 2, TOPK])
        pos_i = sb("pos_i", [P, TOPK], U32)
        pos_ab = sb("pos_ab", [P, 2, TOPK], U32)
        row = sb("row", [P, 2, TOPK])
        idx = [sb(f"idx{i}", [P, TOPK], U32) for i in range(4)]
        cs, gexp, dots, gel, wgt = ([sb(f"{n}{i}", [P, TOPK]) for i in range(2)] for n in ("cs", "gexp", "dots", "gel", "wgt"))
        ncs, gsum, grec = ([sb(f"{n}{i}", [P, 1]) for i in range(2)] for n in ("ncs", "gsum", "grec"))

        s5p = sb("s5p", [P, 3 * S5_TILES])
        lam_r, lam_i, log_step = (s5p[:, S5_TILES * i:S5_TILES * (i + 1)] for i in range(3))
        s5s = sb("s5s", [P, 16, S5_TILES])
        (dt_, lrdt, th, dec, kf, ab, sn_, cs_, ar, ai, mag, kr, ki, thp, cos_n, sin_n) = (s5s[:, i, :] for i in range(16))
        z_last, z_init = sb("z_last", [P, S5_TILES, 2]), sb("z_init", [P, 2, S5_TILES])
        bT = part(0, 2048, a=16)
        cmat = [part(2048 + 384 * i, 384, "p (j v n) -> p j v n", j=4, v=3) for i in range(2)]
        tab = [part(2816 + 1024 * i, 1024, "p (r j s) -> p r j s", r=2, j=4) for i in range(2)]
        turns, whole = part(4864, 512, a=4), part(5376, 512, a=4)
        prod = [[part(5888 + 1024 * i + 512 * v, 512, "p (i r s) -> p i r s", i=2, r=2) for v in range(2)] for i in range(2)]
        zst = part(7936, 512, "p (i r s) -> p i r s", i=2, r=2)
        bs = part(2816, 2048, "p (c r j g n) -> p c r j g n", c=8, r=2, j=4, g=2)
        b_raw = part(4864, 1024, a=2)
        bt1, bt2 = part(5888, 512), part(6400, 512)
        c_raw = sgw[:, :].rearrange("p (r i n) -> p r i n", r=2, i=S5_TILES)
        gate = part(2816, 1024)

        ld_x = [sem(f"ld_x{t}") for t in range(T)]
        ld_cst, ld_sgu, ld_sk, ld_s5, ld_c, ld_b, st_out = (
            sem(n) for n in ("ld_cst", "ld_sgu", "ld_sk", "ld_s5", "ld_c", "ld_b", "st_out"))
        ld_win = [sem(f"ld_win{n}") for n in range(5)]
        ld_w = [sem(f"ld_w{i}") for i in range(2)]
        ld_vec = [sem(f"ld_vec{i}") for i in range(2)]
        got_u = [sem(f"got_u{b}") for b in range(RING)]
        got_v = [sem(f"got_v{b}") for b in range(RING)]
        sq_done, ms_done, sd_done, h_done, nT_done, hT_act, hT_dve, x_done, w_used = (sem(n) for n in (
            "sq_done", "ms_done", "sd_done", "h_done", "nT_done", "hT_act", "hT_dve", "x_done", "w_used"))
        (z_done, z_dve, z_act, sgm_ok, qkT_done, qT_act, kT_dve, lnv_done, lsd_done, g_done, sc_done, nm_done, ex_done,
         p_done, pT_done, pT_act, sp_done, o_done, mix_done, mT_done, mT_act, mT_dve) = (sem(n) for n in (
             "z_done", "z_dve", "z_act", "sgm_ok", "qkT_done", "qT_act", "kT_dve", "lnv_done", "lsd_done", "g_done",
             "sc_done", "nm_done", "ex_done", "p_done", "pT_done", "pT_act", "sp_done", "o_done", "mix_done",
             "mT_done", "mT_act", "mT_dve"))
        (qs_act, qt_done, qt_dve, s_done, s_act, idx_ok, cs_ok, exp_ok, u_free, v_free, gel_ok, wgt_ok, diag_ok) = (
            sem(n) for n in ("qs_act", "qt_done", "qt_dve", "s_done", "s_act", "idx_ok", "cs_ok", "exp_ok", "u_free",
                             "v_free", "gel_ok", "wgt_ok", "diag_ok"))
        (dt_ok, th_ok, dec_ok, thr_ok, cs5_ok, n_ok, csn_ok, b_ok, bT_done, bT_act, whole_ok, frac_ok, tab_ok, xs_done,
         w_ok, d_ok, cz_zero, cz_ok, yc_done, dh_done, ye_ok, g_ok, gT_done, gT_act, gT_dve, bias_ok, sig_ok) = (
             sem(n) for n in (
                 "dt_ok", "th_ok", "dec_ok", "thr_ok", "cs5_ok", "n_ok", "csn_ok", "b_ok", "bT_done", "bT_act",
                 "whole_ok", "frac_ok", "tab_ok", "xs_done", "w_ok", "d_ok", "cz_zero", "cz_ok", "yc_done", "dh_done",
                 "ye_ok", "g_ok", "gT_done", "gT_act", "gT_dve", "bias_ok", "sig_ok"))

        block = ctx.enter_context(nc.Block())

        def att_units(a):
            return (0, [(0, 4), (1, 4)]) if a == 0 else (1, [(4 * a - 4, 2), (4 * a - 3, 2)])

        def bc(ap, dims):
            at = dims.index(None)
            for _ in range(at):
                ap = ap.unsqueeze(1)
            for _ in range(len(dims) - 1 - at):
                ap = ap.unsqueeze(len(ap.shape))
            return ap.to_broadcast([ap.shape[0]] + [ap.shape[1 + at] if d is None else d for d in dims])

        def z_evacs(zi, on_dve):
            return sum((n < 2) == on_dve for _, n in Z_ORDER[:zi])

        @block.sync
        def _(sp):
            vec_read = {0: (h_done, 2), 1: (h_done, 4), 2: (h_done, 5), 3: (dh_done, 1), 4: (bias_ok, 2), 5: (h_done, 6),
                        6: (h_done, 7), 7: (dh_done, 2), 8: (bias_ok, 4)}

            def load_vec(v):
                if v >= 2:
                    sp.wait_ge(*vec_read[v - 2])
                r = VEC_ROW[v]
                sp.dma_start(vec[:, v % 2, :], vecs[r:r + 1, :].to_broadcast([P, D])).then_inc(ld_vec[v % 2], 16)

            blocks = []
            for b, mats in ((0, (w_out, 2)), (0, (wq[0], 4)), (0, (w_out, 2)), (0, (wq[0], 4)), (0, (glu_w, 2)),
                            (0, (wq[1], 4)), (0, (glu_w, 2)), (0, (wq[1], 4))):
                blocks += [(mats[0], n) for n in range(mats[1])]

            def load_w(*which):
                for w in which:
                    if w >= 2:
                        sp.wait_ge(w_used, w - 1)
                    m, n = blocks[w]
                    sp.dma_start(wst[:, w % 2, :, :], m.rearrange("(k p) n -> p k n", p=P)[:, :, n * BANK:(n + 1) * BANK])\
                        .then_inc(ld_w[w % 2], 16)

            w_v = w_in.rearrange("(k p) n -> p k n", p=P)

            def load_win(n):
                sp.dma_start(win[n], w_v[:, :, n * BANK:(n + 1) * BANK]).then_inc(ld_win[n], 16)

            sp.dma_start(x[:, 0, :], x_in[0:P, :]).then_inc(ld_x[0], 16)
            load_vec(0)
            sp.dma_start(cst[:, :], cst_in).then_inc(ld_cst, 16)
            load_win(0)
            load_win(1)
            sp.dma_start(x[:, 1, :], x_in[P:2 * P, :]).then_inc(ld_x[1], 16)
            load_win(2)
            load_win(4)
            load_win(3)
            sp.dma_start(sgw[:, :], sgu_wT).then_inc(ld_sgu, 16)
            sp.dma_start(sg_gain, sgu_g.to_broadcast([P, AW])).then_inc(ld_sgu, 16)
            sp.dma_start(sgb[:, :], sgu_bT).then_inc(ld_sgu, 16)
            sp.dma_start(s5p[:, :], s5_par).then_inc(ld_s5, 16)
            load_w(0, 1)
            load_vec(1)
            sp.dma_start(sk[:, :, :, :], skT).then_inc(ld_sk, 16)
            load_w(2, 3, 4, 5, 6, 7)
            load_vec(2)
            sp.wait_ge(sp_done, T)
            sp.dma_start(c_raw, s5_c).then_inc(ld_c, 16)
            load_w(8, 9)
            load_vec(3)
            load_w(10, 11)
            sp.wait_ge(mix_done, T)
            sp.dma_start(b_raw, s5_b).then_inc(ld_b, 16)
            load_w(12, 13)
            load_vec(4)
            load_vec(5)
            load_w(14, 15)
            load_vec(6)
            load_vec(7)
            load_w(16, 17, 18, 19)
            load_vec(8)
            load_vec(9)
            load_w(20, 21)
            load_vec(10)
            load_w(22, 23)
            for t in range(T):
                sp.wait_ge(h_done, 9 + t)
                sp.dma_start(out[t * P:(t + 1) * P, :], h[:, t, :]).then_inc(st_out, 16)
            sp.wait_ge(st_out, 16 * T)

        @block.gpsimd
        def _(pool):
            pool.wait_ge(ld_sgu, 48)
            sg3 = sgw[:, :].rearrange("p (h i) -> p h i", h=8)
            nc.gpsimd.affine_select(out=sg3, in_=sg3, pattern=[[0, 8], [1, P]], compare_op=ALU.is_ge, fill=0.0, base=0,
                                    channel_multiplier=-1).then_inc(sgm_ok, 1)

            def gather(ring, table, window, s, done):
                nc.gpsimd.indirect_dma_start(
                    out=ring[:, s % RING, :], out_offset=None, in_=table,
                    in_offset=bass.IndirectOffsetOnAxis(ap=idx[window][:, s:s + 1], axis=0)).then_inc(done[s % RING], 16)

            def gathers(n, q, last=False):
                if not last:
                    pool.wait_ge(idx_ok, n + 2)
                for s in range(TOPK):
                    if s % 2 == 0:
                        pool.wait_ge(v_free, n * 16 + (s + 2))
                        if not last:
                            pool.wait_ge(u_free, n * 16 + (s + 18))
                        pool.nop(nofuse=True)
                    gather(ringv, v_tab, q, s, got_v)
                    if not last:
                        gather(ringu, u_tab, (q + 1) % 4, s, got_u)

            pool.wait_ge(idx_ok, 1)
            for s in range(TOPK):
                if s == 0:
                    pool.wait_ge(z_done, 6)
                if s == RING // 2:
                    pool.wait_ge(z_done, 7)
                if s >= RING and s % 2 == 0:
                    pool.wait_ge(u_free, s + 2)
                gather(ringu, u_tab, 0, s, got_u)
            pool.wait_ge(z_done, 9)
            with pool.Fori(0, GROUPS // 4 - 1) as it:
                for q in range(4):
                    gathers(it * 4 + q, q)
            for q in range(4):
                gathers(GROUPS - 4 + q, q, last=(q == 3))

        @block.scalar
        def _(act):
            A = nc.scalar

            def norm(m):
                t = NORM_T[m]
                if m < 2:
                    act.wait_ge(ld_x[t], 16)
                else:
                    act.wait_ge(x_done, 2 * (m - 1))
                A.activation(h[:, t, :], x[:, t, :], ACT.Square, accum_out=ss[:, t:t + 1]).then_inc(sq_done, 1)
                act.wait_ge(ms_done, m + 1)
                A.activation(sd[:, t:t + 1], ms[:, t:t + 1], ACT.Sqrt).then_inc(sd_done, 1)

            def norm_T(m):
                act.wait_ge(nT_done, 2 * m + 1)
                A.activation(hTs[NORM_T[m]][:, 0:4, :], four(0), ACT.Copy).then_inc(hT_act, 1)

            def z(zi):
                t, n = Z_ORDER[zi]
                if n >= 2:
                    act.wait_ge(z_done, zi + 1)
                    dst, fn = {2: (vv, ACT.Copy), 3: (zu, ACT.Gelu_apprx_tanh), 4: (zg, ACT.Gelu_apprx_tanh)}[n]
                    A.activation(dst[:, t, :], ps[:, 4 + zi % 2, :], fn).then_inc(z_act, 1)

            def s5_angle():
                act.wait_ge(ld_s5, 16)
                A.activation(dt_, log_step, ACT.Exp).then_inc(dt_ok, 1)
                act.wait_ge(th_ok, 1)
                A.activation(dec, lrdt, ACT.Exp).then_inc(dec_ok, 1)

            def qk_turn(t):
                act.wait_ge(qkT_done, 2 * t + 1)
                A.activation(aqT[:, :, t * P:(t + 1) * P], four(2), ACT.Copy).then_inc(qT_act, 1)

            def att_a(a):
                t, units = att_units(a)
                keys = P * (t + 1)
                for i, (h0, nh) in enumerate(units):
                    act.wait_ge(nm_done, 2 * a + i + 1)
                    for j in range(nh):
                        c = 8 * t + h0 + 2 * j
                        e = E[i][:, j * keys:(j + 1) * keys]
                        ins = A.activation(e, e, ACT.Exp, bias=negmax[:, c:c + 1])
                    ins.then_inc(ex_done, 1)

            def att_b(a):
                for i in range(2):
                    act.wait_ge(pT_done, 2 * a + i + 1)
                    A.activation(PT[i], ps[:, 2 + i, :], ACT.Copy).then_inc(pT_act, 1)

            def sgu_a(t):
                act.wait_ge(lnv_done, t + 1)
                A.activation(lsd[:, :], var[:, :], ACT.Sqrt).then_inc(lsd_done, 1)

            def mix_T(t):
                act.wait_ge(mT_done, 2 * t + 1)
                A.activation(hTs[t][:, 0:4, :], four(0), ACT.Copy).then_inc(mT_act, 1)

            def q_in(p, b):
                act.wait_ge(w_used, Q_BLK[p] + b + 1)
                if 4 * p + b > 0:
                    act.wait_ge(qt_done, 4 * p + b)
                A.activation(qs, ps[:, 2, :], ACT.Copy).then_inc(qs_act, 1)

            def q_score(p, b):
                act.wait_ge(s_done, 4 * p + b + 1)
                if p > 0:
                    act.wait_ge(idx_ok, PH * (p - 1) + 2 * b + 2)
                A.activation(S[:, 2 * b:2 * b + 2, :], ps[:, 2, :].rearrange("p (a s) -> p a s", a=2),
                             ACT.Copy).then_inc(s_act, 1)

            def s5_setup():
                act.wait_ge(thr_ok, 1)
                A.activation(ab, th, ACT.Abs)
                A.activation(sn_, th, ACT.Sin)
                act.drain()
                A.activation(cs_, ab, ACT.Sin, bias=half_pi, scale=-1.0).then_inc(cs5_ok, 1)
                act.wait_ge(n_ok, 1)
                A.activation(sin_n, kf, ACT.Sin, scale=-TURN)
                A.activation(cos_n, kf, ACT.Abs)
                act.drain()
                A.activation(cos_n, cos_n, ACT.Sin, bias=half_pi, scale=-TURN).then_inc(csn_ok, 1)
                for b in range(4):
                    act.wait_ge(bT_done, b + 1)
                    A.activation(bT[:, 4 * b:4 * b + 4, :], four(b), ACT.Copy).then_inc(bT_act, 1)

            def turn_counts(ci):
                c = ci % KC
                for j in range(4):
                    A.activation(turns[:, j, :], time_row, ACT.Copy, scale=thp[:, 4 * c + j:4 * c + j + 1])
                act.drain()
                A.activation(whole, turns, ACT.Copy, bias=ROUND).then_inc(whole_ok, 1)

            def tables(ci):
                act.wait_ge(frac_ok, ci + 1)
                if ci >= 2:
                    act.wait_ge(d_ok, 4 * (ci - 1))
                A.activation(tab[ci % 2][:, 1, :, :], whole, ACT.Sin, scale=-TURN)
                A.activation(tab[ci % 2][:, 0, :, :], whole, ACT.Abs)
                act.drain()
                A.activation(tab[ci % 2][:, 0, :, :], tab[ci % 2][:, 0, :, :], ACT.Sin, bias=half_pi,
                             scale=-TURN).then_inc(tab_ok, 1)
                act.drain()

            def s5(t, pr):
                c = pr // 2
                ci = KC * t + c
                if pr % 2:
                    if c + 1 < KC:
                        tables(ci + 1)
                    return
                if c == 0:
                    act.wait_ge(hT_act, 5 + 2 * t)
                    turn_counts(ci)
                    tables(ci)
                    if t == 0:
                        act.wait_ge(ld_c, 16)
                        act.wait_ge(cz_zero, 2)
                if c + 1 < KC:
                    turn_counts(ci + 1)
                if ci >= 2:
                    act.wait_ge(yc_done, 2 * (ci - 1))
                for g in range(2):
                    half = slice(64 * g, 64 * g + 64)
                    for v, (r, sign) in enumerate(((0, 1.0), (0, -1.0), (1, -1.0))):
                        A.activation(cmat[ci % 2][half, :, v, 16 * g:16 * g + 16], c_raw[half, r, 4 * c:4 * c + 4, :],
                                     ACT.Copy, scale=sign).then_inc(cz_ok, 1)

            def s5_end(t):
                act.wait_ge(ye_ok, 2 * (t + 1))
                A.activation(h[:, t, :], h[:, t, :], ACT.Gelu_apprx_tanh).then_inc(g_ok, 1)

            def gate_T(t):
                act.wait_ge(gT_done, 2 * t + 1)
                A.activation(hTs[t][:, 0:4, :], four(0), ACT.Copy).then_inc(gT_act, 1)

            def glu(t, b):
                act.wait_ge(bias_ok, 2 * t + b + 1)
                g = gate[:, b * BANK:(b + 1) * BANK]
                A.activation(g, g, ACT.Sigmoid).then_inc(sig_ok, 1)

            def gate_exp(n):
                act.wait_ge(cs_ok, n + 1)
                if n >= 2:
                    act.wait_ge(wgt_ok, n - 1)
                A.activation(gexp[n % 2][:, :], cs[n % 2][:, :], ACT.Exp, bias=ncs[n % 2][:, :],
                             accum_out=gsum[n % 2][:, :]).then_inc(exp_ok, 1)

            def gelu(n):
                act.wait_ge(u_free, 16 * (n + 1) + RING)
                A.activation(gel[n % 2][:, :], dots[n % 2][:, :], ACT.Gelu_apprx_tanh).then_inc(gel_ok, 1)

            def diagonals(n):
                if n == 0:
                    act.wait_ge(z_done, len(Z_ORDER))
                if n >= 2:
                    act.wait_ge(v_free, 16 * (n - 1) + RING)
                act.wait_ge(wgt_ok, n + 1)
                for s in range(TOPK):
                    A.activation(diag[n % 2][:, s, :], ident, ACT.Copy, scale=wgt[n % 2][:, s:s + 1]).then_inc(diag_ok, 1)

            stage = dict(norm=norm, norm_T=norm_T, z=z, s5_angle=s5_angle, qk_turn=qk_turn, att_a=att_a, att_b=att_b,
                         sgu_a=sgu_a, mix_T=mix_T, gate_T=gate_T,
                         q_in=q_in, q_score=q_score, s5_setup=s5_setup, s5=s5, s5_end=s5_end, glu=glu)

            def run(stages):
                for name, *args in stages:
                    if name in stage:
                        stage[name](*args)

            run(PRELUDE)
            gate_exp(0)
            for n in range(GROUPS):
                for s in range(TOPK):
                    run(WORK[n].get(s, []))
                    if s == ROUTE_AT and n + 1 < GROUPS:
                        gate_exp(n + 1)
                gelu(n)
                diagonals(n)
            run(LAST)

        @block.tensor
        def _(pe):
            PE = nc.tensor

            moved = {}

            def banks_2_3():
                for what in moved:
                    pe.wait_ge(*moved[what])

            def wait_hT(m):
                pe.wait_ge(hT_act, m + 1)
                pe.wait_ge(hT_dve, m + 1)

            def turn(bank, src, done):
                for a in range(4):
                    ins = PE.transpose(ps[:, bank, a * P:(a + 1) * P], src[:, a * P:(a + 1) * P], ident)
                ins.then_inc(done, 1)

            def product(bank, lhs, rhs, done):
                for k in range(KC):
                    ins = PE.matmul(ps[:, bank, :], lhs[:, k, :], rhs[:, k, :], start=(k == 0), stop=(k == KC - 1))
                ins.then_inc(done, 1)

            def stream(bank, t, w):
                pe.wait_ge(ld_w[w % 2], 16 * (w // 2 + 1))
                product(bank, hTs[t], wst[:, w % 2, :, :], w_used)

            def norm_T(m):
                if m == 0:
                    pe.wait_ge(ld_cst, 16)
                if m == 1:
                    pe.wait_ge(p_done, 2)
                pe.wait_ge(h_done, m + 1)
                for b in range(2):
                    turn(b, h[:, NORM_T[m], b * BANK:(b + 1) * BANK], nT_done)

            def z(zi):
                t, n = Z_ORDER[zi]
                wait_hT(t)
                pe.wait_ge(ld_win[n], 16)
                if zi >= 2:
                    on_dve = Z_ORDER[zi - 2][1] < 2
                    pe.wait_ge(z_dve if on_dve else z_act, z_evacs(zi - 1, on_dve))
                product(4 + zi % 2, hTs[t], win[n], z_done)

            def qk_turn(t):
                pe.wait_ge(z_dve, 2 * (t + 1))
                if t == 1:
                    pe.wait_ge(pT_act, 2)
                    banks_2_3()
                for w in range(2):
                    turn(2 + w, qk[w], qkT_done)
                moved["q"], moved["k"] = (qT_act, t + 1), (kT_dve, t + 1)

            def att_a(a):
                t, units = att_units(a)
                keys = P * (t + 1)
                pe.wait_ge(qT_act, t + 1)
                pe.wait_ge(kT_dve, t + 1)
                for i, (h0, nh) in enumerate(units):
                    for j in range(nh):
                        hd = h0 + 2 * j
                        r = slice(HD * (hd % 2), HD * (hd % 2) + HD)
                        ins = PE.matmul(ps[:, i, j * keys:(j + 1) * keys], aqT[r, hd // 2, t * P:(t + 1) * P],
                                        akT[r, hd // 2, 0:keys], start=True, stop=True)
                    ins.then_inc(sc_done, 1)

            def att_b(a):
                t, units = att_units(a)
                banks_2_3()
                for i in range(2):
                    pe.wait_ge(p_done, 2 * a + i + 1)
                    turn(2 + i, E[i], pT_done)
                for i, (h0, nh) in enumerate(units):
                    pe.wait_ge(pT_act, 2 * a + i + 1)
                    for j in range(nh):
                        hd = h0 + 2 * j
                        for kt in range(t + 1):
                            blk = j * (t + 1) + kt
                            ins = PE.matmul(ps[:, 6, hd * HD:(hd + 1) * HD], PT[i][:, blk * P:(blk + 1) * P],
                                            vv[:, kt, hd * HD:(hd + 1) * HD], start=(kt == 0), stop=(kt == t))
                ins.then_inc(o_done, 1)

            def sgu_b(t):
                pe.wait_ge(sgm_ok, 1)
                pe.wait_ge(g_done, t + 1)
                for g in range(8):
                    ins = PE.matmul(ps[:, 7, g * 64:(g + 1) * 64], sgw[:, g * P:(g + 1) * P], zg[:, t, g * 64:(g + 1) * 64],
                                    start=True, stop=True)
                ins.then_inc(sp_done, 1)

            def mix_T(t):
                pe.wait_ge(mix_done, t + 1)
                if t == 0:
                    wait_hT(1)
                for b in range(2):
                    turn(b, h[:, t, b * BANK:(b + 1) * BANK], mT_done)

            def w_out_(t, b):
                pe.wait_ge(mT_act, t + 1)
                pe.wait_ge(mT_dve, t + 1)
                banks_2_3()
                stream(2 + b, t, WOUT_BLK[t] + b)

            def q_in(p, b):
                wait_hT(Q_NORM[p])
                banks_2_3()
                stream(2, p % T, Q_BLK[p] + b)

            def q_turn(p, b):
                pe.wait_ge(qs_act, 4 * p + b + 1)
                turn(3, qs, qt_done)

            def q_score(p, b):
                pe.wait_ge(qt_dve, 4 * p + b + 1)
                pe.wait_ge(ld_sk, 16)
                for a in range(4):
                    ins = PE.matmul(ps[:, 2, a * P:(a + 1) * P], qT[:, a, :], sk[:, p // T, a % 2, :], start=True, stop=True)
                ins.then_inc(s_done, 1)
                moved["scores"] = (s_act, 4 * p + b + 1)

            def s5_setup():
                pe.wait_ge(b_ok, 1)
                banks_2_3()
                for b in range(4):
                    for a in range(4):
                        c, r = (4 * b + a) // 2, a % 2
                        ins = PE.transpose(ps[:, b, a * P:(a + 1) * P],
                                           bs[:, c, r, :, :, :].rearrange("p j g n -> p (j g n)"), ident)
                    ins.then_inc(bT_done, 1)
                moved["s5"] = (bT_act, 4)

            def s5_in(t, pr):
                pi = 16 * t + pr
                if pi >= 2:
                    pe.wait_ge(w_ok, pi - 1)
                c = pr // 2
                for j in (2 * (pr % 2), 2 * (pr % 2) + 1):
                    rows = slice(32 * j, 32 * j + 32)
                    for r in range(2):
                        ins = PE.matmul(ps[:, j, r * P:(r + 1) * P], bT[rows, 2 * c + r, :], hTs[t][rows, c, :],
                                        start=True, stop=True)
                ins.then_inc(xs_done, 1)

            def s5_out(t, pr):
                pi = 16 * t + pr
                c = pr // 2
                pe.wait_ge(d_ok, 2 * (pi + 1))
                pe.wait_ge(cz_ok, 6 * (KC * t + c + 1))
                by_cos, by_sin = prod[pi % 2]
                for i in range(2):
                    j = 2 * (pr % 2) + i
                    tile = 4 * c + j
                    o = ps[:, 4 + 2 * t + tile // 16, 32 * (tile % 16):32 * (tile % 16) + 32]
                    m = cmat[c % 2]
                    terms = ((by_cos[:, i, 0, :], 0), (by_sin[:, i, 1, :], 1), (by_sin[:, i, 0, :], 2), (by_cos[:, i, 1, :], 2))
                    for q, (d, v) in enumerate(terms):
                        ins = PE.matmul(o, d, m[:, j, v, :], start=(q == 0), stop=(q == 3))
                ins.then_inc(yc_done, 1)

            def s5(t, pr):
                if pr == 0:
                    wait_hT(4 + 2 * t)
                    pe.wait_ge(bT_act, 4)
                    banks_2_3()
                    s5_in(t, 0)
                if pr + 1 < 16:
                    s5_in(t, pr + 1)
                if pr > 0:
                    s5_out(t, pr - 1)

            def s5_end(t):
                s5_out(t, 15)

            def gate_T(t):
                pe.wait_ge(g_ok, t + 1)
                for b in range(2):
                    turn(b, h[:, t, b * BANK:(b + 1) * BANK], gT_done)

            def glu(t, b):
                pe.wait_ge(gT_act, t + 1)
                pe.wait_ge(gT_dve, t + 1)
                banks_2_3()
                stream(2 + b, t, GLU_BLK[t] + b)

            def experts(n, work):
                t = n // PH % T
                if n == 0:
                    pe.wait_ge(z_act, z_evacs(len(Z_ORDER), False))
                for s in range(TOPK):
                    run(work.get(s, []))
                    pe.wait_ge(diag_ok, 16 * n + s + 1)
                    pe.wait_ge(got_v[s % RING], 16 * (2 * n + 1 + s // RING))
                    for b in range(2):
                        ins = PE.matmul(ps[:, 4 + 2 * t + b, :], diag[n % 2][:, s, :], ringv[:, s % RING, b * BANK:(b + 1) * BANK],
                                        start=(n % PH == 0 and s == 0), stop=(n % PH == PH - 1 and s == TOPK - 1))
                    ins.then_inc(v_free, 1)

            stage = dict(norm_T=norm_T, z=z, qk_turn=qk_turn, att_a=att_a, att_b=att_b, sgu_b=sgu_b, mix_T=mix_T, w_out=w_out_,
                         q_in=q_in, q_turn=q_turn, q_score=q_score, s5_setup=s5_setup, s5=s5,
                         s5_end=s5_end, gate_T=gate_T, glu=glu)

            def run(stages):
                for name, *args in stages:
                    if name in stage:
                        stage[name](*args)

            run(PRELUDE)
            for slot in sorted(WORK[0]):
                run(WORK[0][slot])
            for n in range(1, GROUPS):
                experts(n - 1, WORK[n])
            experts(GROUPS - 1, {})

        @block.vector
        def _(dve):
            V = nc.vector

            def norm(m):
                t = NORM_T[m]
                dve.wait_ge(sq_done, m + 1)
                V.tensor_scalar(ms[:, t:t + 1], ss[:, t:t + 1], 1.0 / D, RMS_EPS, ALU.mult, ALU.add).then_inc(ms_done, 1)
                dve.wait_ge(sd_done, m + 1)
                V.reciprocal(rstd[:, t:t + 1], sd[:, t:t + 1])
                dve.drain()
                v = NORM_VEC[m]
                dve.wait_ge(ld_vec[v % 2], 16 * (v // 2 + 1))
                V.scalar_tensor_tensor(h[:, t, :], x[:, t, :], rstd[:, t:t + 1], vec[:, v % 2, :], ALU.mult,
                                       ALU.mult).then_inc(h_done, 1)

            def norm_T(m):
                dve.wait_ge(nT_done, 2 * m + 2)
                V.tensor_copy(hTs[NORM_T[m]][:, 4:8, :], four(1)).then_inc(hT_dve, 1)

            def residual(t, b, term):
                xs = x[:, t, b * BANK:(b + 1) * BANK]
                V.tensor_tensor(xs, xs, term, ALU.add).then_inc(x_done, 1)

            def z(zi):
                t, w = Z_ORDER[zi]
                if w >= 2:
                    return
                dve.wait_ge(z_done, zi + 1)
                z4 = ps[:, 4 + zi % 2, :].rearrange("p (h a d) -> p h a d", h=HEADS, a=2)
                a4 = rot_a.rearrange("p (h a d) -> p h a d", h=HEADS, a=2)
                b4 = rot_b.rearrange("p (h a d) -> p h a d", h=HEADS, a=2)
                V.tensor_tensor(a4, z4, bc(cos_t[:, t, :], [HEADS, 2, None]), ALU.mult)
                V.tensor_tensor(b4[:, :, 0, :], z4[:, :, 1, :], bc(nsin_t[:, t, :], [HEADS, None]), ALU.mult)
                V.tensor_tensor(b4[:, :, 1, :], z4[:, :, 0, :], bc(sin_t[:, t, :], [HEADS, None]), ALU.mult)
                dve.drain()
                if t == 1:
                    dve.wait_ge(qkT_done, 2)
                V.tensor_tensor(qk[w], rot_a, rot_b, ALU.add).then_inc(z_dve, 1)
                dve.drain()

            def s5_angle():
                dve.wait_ge(dt_ok, 1)
                V.tensor_tensor(th, lam_i, dt_, ALU.mult)
                V.tensor_tensor(lrdt, lam_r, dt_, ALU.mult).then_inc(th_ok, 1)
                dve.drain()
                V.tensor_scalar(kf, th, INV_TWO_PI, ROUND, ALU.mult, ALU.add)
                dve.drain()
                V.tensor_scalar(kf, kf, ROUND, None, ALU.subtract)
                dve.drain()
                V.scalar_tensor_tensor(th, kf, -TWO_PI_HI, th, ALU.mult, ALU.add)
                dve.drain()
                V.scalar_tensor_tensor(th, kf, -TWO_PI_LO, th, ALU.mult, ALU.add)
                dve.drain()
                V.tensor_scalar(th, th, PI_BELOW, -PI_BELOW, ALU.min, ALU.max).then_inc(thr_ok, 1)
                dve.drain()
                V.tensor_scalar(thp, th, INV_TWO_PI, None, ALU.mult)
                dve.drain()

            def qk_turn(t):
                dve.wait_ge(qkT_done, 2 * t + 2)
                V.tensor_copy(akT[:, :, t * P:(t + 1) * P], four(3)).then_inc(kT_dve, 1)

            def att_a(a):
                t, units = att_units(a)
                for i, (h0, nh) in enumerate(units):
                    cols = slice(8 * t + h0, 8 * t + h0 + 2 * nh - 1, 2)
                    dve.wait_ge(sc_done, 2 * a + i + 1)
                    e3 = E[i].rearrange("p (h k) -> p h k", h=nh)
                    V.scalar_tensor_tensor(e3, ps[:, i, :].rearrange("p (h k) -> p h k", h=nh), SCALE,
                                           bc(negm[t], [nh, None]), ALU.mult, ALU.add)
                    dve.drain()
                    V.tensor_reduce(negmax[:, cols], e3, AX.X, ALU.max, negate=True).then_inc(nm_done, 1)
                for i, (h0, nh) in enumerate(units):
                    cols = slice(8 * t + h0, 8 * t + h0 + 2 * nh - 1, 2)
                    dve.wait_ge(ex_done, 2 * a + i + 1)
                    e3 = E[i].rearrange("p (h k) -> p h k", h=nh)
                    V.tensor_tensor(e3, e3, bc(count[t], [nh, None]), ALU.mult)
                    dve.drain()
                    V.tensor_reduce(den[:, cols], e3, AX.X, ALU.add).then_inc(p_done, 1)

            def sgu_a(t):
                dve.wait_ge(z_act, 2 + 3 * t)
                g3 = zg[:, t, :].rearrange("p (g d) -> p g d", g=8)
                s3 = sg_tmp.rearrange("p (g d) -> p g d", g=8)
                V.tensor_reduce(mu[:, :], g3, AX.X, ALU.add)
                dve.drain()
                V.scalar_tensor_tensor(g3, bc(mu[:, :], [None, 64]), -1.0 / 64, g3, ALU.mult, ALU.add)
                dve.drain()
                V.tensor_tensor(s3, g3, g3, ALU.mult)
                dve.drain()
                V.tensor_reduce(var[:, :], s3, AX.X, ALU.add)
                dve.drain()
                V.tensor_scalar(var[:, :], var[:, :], 1.0 / 64, LN_EPS, ALU.mult, ALU.add).then_inc(lnv_done, 1)
                dve.wait_ge(lsd_done, t + 1)
                V.reciprocal(lrs[:, :], lsd[:, :])
                dve.drain()
                V.tensor_tensor(g3, g3, bc(lrs[:, :], [None, 64]), ALU.mult)
                dve.drain()
                dve.wait_ge(ld_sgu, 48)
                V.tensor_tensor(zg[:, t, :], zg[:, t, :], sg_gain, ALU.mult).then_inc(g_done, 1)

            def sgu_b(t):
                dve.wait_ge(sp_done, t + 1)
                dve.wait_ge(z_act, 3 + 3 * t)
                s3 = sg_tmp.rearrange("p (g d) -> p g d", g=8)
                V.tensor_tensor(s3, ps[:, 7, :].rearrange("p (g d) -> p g d", g=8), bc(sgb[:, :], [None, 64]), ALU.add)
                dve.drain()
                V.tensor_tensor(h[:, t, AW:2 * AW], sg_tmp, zu[:, t, :], ALU.mult)
                dve.drain()

            def mix(t):
                dve.wait_ge(o_done, (1, 3)[t])
                V.reciprocal(rden[:, 8 * t:8 * t + 8], den[:, 8 * t:8 * t + 8])
                dve.drain()
                V.tensor_tensor(h[:, t, 0:AW].rearrange("p (h d) -> p h d", h=HEADS),
                                ps[:, 6, :].rearrange("p (h d) -> p h d", h=HEADS),
                                bc(rden[:, 8 * t:8 * t + 8], [None, HD]), ALU.mult).then_inc(mix_done, 1)

            def mix_T(t):
                dve.wait_ge(mT_done, 2 * t + 2)
                V.tensor_copy(hTs[t][:, 4:8, :], four(1)).then_inc(mT_dve, 1)

            def w_out_(t, b):
                dve.wait_ge(w_used, WOUT_BLK[t] + b + 1)
                residual(t, b, ps[:, 2 + b, :])

            def q_turn(p, b):
                dve.wait_ge(qt_done, 4 * p + b + 1)
                if 4 * p + b > 0:
                    dve.wait_ge(s_done, 4 * p + b)
                V.tensor_copy(qT, four(3)).then_inc(qt_dve, 1)

            def y_sum(r):
                t = (0, 1, 0, 1)[(2, 4, 6, 7).index(r)]
                phase = (2, 4, 6, 7).index(r)
                dve.wait_ge(v_free, RING + 16 * PH * (phase + 1))
                for b in range(2):
                    residual(t, b, ps[:, 4 + 2 * t + b, :])

            def s5_setup():
                V.memset(bs, 0.0)
                V.memset(cmat[0], 0.0).then_inc(cz_zero, 1)
                V.memset(cmat[1], 0.0).then_inc(cz_zero, 1)
                V.tensor_scalar(mag, thp, float(P), None, ALU.mult)
                dve.drain()
                V.tensor_scalar(kf, mag, ROUND, None, ALU.add)
                dve.drain()
                V.scalar_tensor_tensor(kf, kf, ROUND, mag, ALU.subtract, ALU.subtract).then_inc(n_ok, 1)
                dve.wait_ge(cs5_ok, 1)
                dve.wait_ge(dec_ok, 1)
                dve.drain()
                V.tensor_tensor(ar, dec, cs_, ALU.mult)
                V.tensor_tensor(ai, dec, sn_, ALU.mult)
                V.tensor_tensor(mag, lam_r, lam_r, ALU.mult)
                V.tensor_tensor(lrdt, lam_i, lam_i, ALU.mult)
                dve.drain()
                V.tensor_tensor(mag, mag, lrdt, ALU.add)
                V.tensor_scalar(ar, ar, 1.0, None, ALU.subtract)
                dve.drain()
                V.reciprocal(mag, mag)
                V.tensor_tensor(kr, ar, lam_r, ALU.mult)
                V.tensor_tensor(lrdt, ai, lam_i, ALU.mult)
                V.tensor_tensor(ki, ai, lam_r, ALU.mult)
                V.tensor_tensor(ab, ar, lam_i, ALU.mult)
                dve.drain()
                V.tensor_tensor(kr, kr, lrdt, ALU.add)
                V.tensor_tensor(ki, ki, ab, ALU.subtract)
                dve.drain()
                V.tensor_tensor(kr, kr, mag, ALU.mult)
                V.tensor_tensor(ki, ki, mag, ALU.mult)
                dve.drain()
                dve.wait_ge(ld_b, 16)
                for r in range(2):
                    for dst, k_, r_ in ((bt1, kr, r), (bt2, ki, 1 - r)):
                        V.tensor_tensor(dst.rearrange("p (i n) -> p i n", i=S5_TILES), bc(k_, [None, 16]),
                                        b_raw[:, r_, :].rearrange("p (i n) -> p i n", i=S5_TILES), ALU.mult)
                    dve.drain()
                    for g in range(2):
                        half = slice(64 * g, 64 * g + 64)
                        ins = V.tensor_tensor(bs[half, :, r, :, g, :],
                                              bt1[half, :].rearrange("p (c j n) -> p c j n", c=8, j=4),
                                              bt2[half, :].rearrange("p (c j n) -> p c j n", c=8, j=4),
                                              (ALU.subtract, ALU.add)[r])
                    if r == 0:
                        dve.drain()
                ins.then_inc(b_ok, 1)

            def fraction(ci):
                dve.wait_ge(whole_ok, ci + 1)
                V.scalar_tensor_tensor(whole, whole, ROUND, turns, ALU.subtract, ALU.subtract).then_inc(frac_ok, 1)

            def s5_pair(t, pr):
                pi, c = 16 * t + pr, pr // 2
                js = slice(2 * (pr % 2), 2 * (pr % 2) + 2)
                cos, sin = (bc_pair(tab[c % 2][:, r, js, :]) for r in range(2))
                by_cos, by_sin = prod[pi % 2]
                dve.wait_ge(xs_done, pi + 1)
                dve.wait_ge(tab_ok, KC * t + c + 1)
                if pi >= 2:
                    dve.wait_ge(yc_done, pi - 1)
                x4 = ps[:, js, 0:2 * P].rearrange("p i (r s) -> p i r s", r=2)
                V.tensor_tensor(by_cos, x4, cos, ALU.mult)
                V.tensor_tensor(by_sin, x4, sin, ALU.mult)
                dve.drain()
                V.tensor_tensor(by_cos[:, :, 0, :], by_cos[:, :, 0, :], by_sin[:, :, 1, :], ALU.add)
                V.tensor_tensor(by_cos[:, :, 1, :], by_cos[:, :, 1, :], by_sin[:, :, 0, :], ALU.subtract).then_inc(w_ok, 1)
                dve.drain()
                for i in range(2):
                    tile = 4 * c + js.start + i
                    for r in range(2):
                        V.tensor_tensor_scan(zst[:, i, r, :], dec[:, tile:tile + 1].to_broadcast([P, P]), by_cos[:, i, r, :],
                                             z_init[:, r, tile:tile + 1] if t else 0.0, ALU.mult, ALU.add)
                dve.drain()
                V.tensor_tensor(by_cos, zst, cos, ALU.mult).then_inc(d_ok, 1)
                V.tensor_tensor(by_sin, zst, sin, ALU.mult).then_inc(d_ok, 1)
                if t == 0:
                    tile = 4 * c + js.start
                    V.tensor_copy(z_last[:, tile:tile + 2, :], zst[:, :, :, P - 1])
                dve.drain()

            def bc_pair(ap):
                return ap.unsqueeze(2).to_broadcast([P, 2, 2, P])

            def s5(t, pr):
                ci = KC * t + pr // 2
                if pr == 0:
                    fraction(ci)
                    if t == 1:
                        dve.wait_ge(csn_ok, 1)
                        zr, zi = z_last[:, :, 0], z_last[:, :, 1]
                        V.tensor_tensor(kr, cos_n, zr, ALU.mult)
                        V.tensor_tensor(ki, sin_n, zi, ALU.mult)
                        V.tensor_tensor(ar, sin_n, zr, ALU.mult)
                        V.tensor_tensor(ai, cos_n, zi, ALU.mult)
                        dve.drain()
                        V.tensor_tensor(z_init[:, 0, :], kr, ki, ALU.subtract)
                        V.tensor_tensor(z_init[:, 1, :], ar, ai, ALU.add)
                if pr % 2 and pr + 1 < 16:
                    fraction(ci + 1)
                s5_pair(t, pr)

            def s5_end(t):
                v = D_VEC[t]
                dve.wait_ge(ld_vec[v % 2], 16 * (v // 2 + 1))
                V.tensor_tensor(h[:, t, :], h[:, t, :], vec[:, v % 2, :], ALU.mult).then_inc(dh_done, 1)
                dve.drain()
                dve.wait_ge(yc_done, 16 * (t + 1))
                for b in range(2):
                    hs = h[:, t, b * BANK:(b + 1) * BANK]
                    V.tensor_tensor(hs, hs, ps[:, 4 + 2 * t + b, :], ALU.add).then_inc(ye_ok, 1)

            def gate_T(t):
                dve.wait_ge(gT_done, 2 * t + 2)
                V.tensor_copy(hTs[t][:, 4:8, :], four(1)).then_inc(gT_dve, 1)

            def glu(t, b):
                v = BIAS_VEC[t]
                cols = slice(b * BANK, (b + 1) * BANK)
                dve.wait_ge(ld_vec[v % 2], 16 * (v // 2 + 1))
                dve.wait_ge(w_used, GLU_BLK[t] + b + 1)
                V.tensor_tensor(gate[:, cols], ps[:, 2 + b, :], vec[:, v % 2, cols], ALU.add).then_inc(bias_ok, 1)
                dve.wait_ge(sig_ok, 2 * t + b + 1)
                V.tensor_tensor(gate[:, cols], gate[:, cols], h[:, t, cols], ALU.mult)
                dve.drain()
                residual(t, b, gate[:, cols])

            def route(n):
                keys = S[:, n % PH, :].rearrange("p (a k) -> p a k", a=2)
                top_cs = cs[n % 2]
                dve.wait_ge(s_act, 4 * (n // PH) + n % PH // 2 + 1)
                for p in range(2):
                    V.max(top[:, p, 0:8], keys[:, p, :])
                dve.drain()
                for p in range(2):
                    V.max_index(top_i[:, p, 0:8], top[:, p, 0:8], keys[:, p, :])
                    V.match_replace(key_b[:, p, :], top[:, p, 0:8], keys[:, p, :], LOWEST)
                dve.drain()
                for p in range(2):
                    V.max(top[:, p, 8:16], key_b[:, p, :])
                dve.drain()
                for p in range(2):
                    V.max_index(top_i[:, p, 8:16], top[:, p, 8:16], key_b[:, p, :])
                V.tensor_tensor(cand_a[:, :].rearrange("p (a b) -> p a b", a=TOPK), bc(top[:, 0, :], [None, TOPK]),
                                bc(top[:, 1, :], [TOPK, None]), ALU.add)
                dve.drain()
                V.max(top_cs[:, 0:8], cand_a[:, :])
                V.tensor_scalar(top_f[:, 0, :], top_i[:, 0, :], float(NK * (n // (T * PH))), None, ALU.add)
                V.tensor_copy(top_f[:, 1, :], top_i[:, 1, :])
                dve.drain()
                V.max_index(pos_i[:, 0:8], top_cs[:, 0:8], cand_a[:, :])
                V.match_replace(cand_b[:, :], top_cs[:, 0:8], cand_a[:, :], LOWEST)
                V.tensor_scalar(ncs[n % 2][:, :], top_cs[:, 0:1], -1.0, None, ALU.mult)
                dve.drain()
                V.max(top_cs[:, 8:16], cand_b[:, :])
                dve.drain()
                V.max_index(pos_i[:, 8:16], top_cs[:, 8:16], cand_b[:, :]).then_inc(cs_ok, 1)
                dve.drain()
                V.tensor_scalar(pos_ab[:, 0, :], pos_i[:, :], 4, None, ALU.logical_shift_right)
                V.tensor_scalar(pos_ab[:, 1, :], pos_i[:, :], 15, None, ALU.bitwise_and)
                dve.drain()
                hot = [c[:, :].rearrange("p (a b) -> p a b", a=TOPK) for c in (cand_a, cand_b)]
                for p in range(2):
                    V.tensor_tensor(hot[p], bc(pos_ab[:, p, :], [None, TOPK]), bc(iota16, [TOPK, None]), ALU.is_equal)
                dve.drain()
                for p in range(2):
                    V.tensor_tensor(hot[p], hot[p], bc(top_f[:, p, :], [TOPK, None]), ALU.mult)
                dve.drain()
                for p in range(2):
                    V.tensor_reduce(row[:, p, :], hot[p], AX.X, ALU.add)
                dve.drain()
                if n >= 4:
                    dve.wait_ge(v_free, 16 * (n - 3) + RING)
                V.scalar_tensor_tensor(idx[n % 4][:, :], row[:, 0, :], float(NK), row[:, 1, :], ALU.mult,
                                       ALU.add).then_inc(idx_ok, 1)

            def dot_products(n):
                t = n // PH % T
                for s in range(TOPK):
                    run(WORK[n].get(s, []))
                    if s == ROUTE_AT and n + 1 < GROUPS:
                        route(n + 1)
                    u = ringu[:, s % RING, :]
                    dve.wait_ge(got_u[s % RING], 16 * (2 * n + 1 + s // RING))
                    V.tensor_tensor_reduce(out=u, in0=u, in1=h[:, t, :], scale=1.0, scalar=0.0, op0=ALU.mult, op1=ALU.add,
                                           accum_out=dots[n % 2][:, s:s + 1]).then_inc(u_free, 1)

            def weights(n):
                i = n % 2
                dve.wait_ge(exp_ok, n + 1)
                V.reciprocal(grec[i][:, :], gsum[i][:, :])
                dve.drain()
                dve.wait_ge(gel_ok, n + 1)
                V.scalar_tensor_tensor(wgt[i][:, :], gexp[i][:, :], grec[i][:, :], gel[i][:, :], ALU.mult,
                                       ALU.mult).then_inc(wgt_ok, 1)

            stage = dict(norm=norm, norm_T=norm_T, z=z, s5_angle=s5_angle, qk_turn=qk_turn, att_a=att_a, sgu_a=sgu_a,
                         sgu_b=sgu_b, mix=mix, mix_T=mix_T, gate_T=gate_T, w_out=w_out_, q_turn=q_turn, y_sum=y_sum, s5_setup=s5_setup, s5=s5, s5_end=s5_end, glu=glu)

            def run(stages):
                for name, *args in stages:
                    if stage.get(name):
                        stage[name](*args)

            V.memset(rden[:, 0:1], 0.0).then_inc(u_free, RING)
            V.memset(rden[:, 1:2], 0.0).then_inc(v_free, RING)
            run(PRELUDE)
            route(0)
            for n in range(GROUPS):
                dot_products(n)
                weights(n)
            run(LAST)


def constants():
    import numpy as np
    c = np.zeros((P, C_ALL), np.float32)
    c[:, C_ID:C_ID + P] = np.eye(P, dtype=np.float32)
    tok = np.arange(SEQ)
    d = tok[:, None] - tok[None, :]
    cnt = ((d >= 0) & (d <= 128)).astype(np.float32)
    for window, dil in ((512, 4), (2048, 16)):
        cnt += ((d >= 0) & (d <= window) & (d % dil == 0)).astype(np.float32)
    neg = np.where(cnt > 0, np.float32(0), np.float32(-1e37))
    half = HD // 2
    inv = np.power(np.float32(10000.0), (-2.0 * np.arange(half, dtype=np.float32) / HD).astype(np.float32))
    ang = tok.astype(np.float32)[:, None] * inv.astype(np.float32)[None, :]
    for t in range(T):
        r = slice(t * P, (t + 1) * P)
        keys = P * (t + 1)
        c[:, C_CNT + P * t:C_CNT + P * t + keys] = cnt[r, :keys]
        c[:, C_NEG + P * t:C_NEG + P * t + keys] = neg[r, :keys]
        c[:, C_COS + half * t:C_COS + half * (t + 1)] = np.cos(ang[r])
        c[:, C_SIN + half * t:C_SIN + half * (t + 1)] = np.sin(ang[r])
        c[:, C_NSIN + half * t:C_NSIN + half * (t + 1)] = -np.sin(ang[r])
    c[:, C_IOTA:C_IOTA + 16] = np.arange(16)
    c[:, C_TIME:C_TIME + P] = np.arange(P)
    c[:, C_HPI] = np.pi / 2
    return c


def kernel(x, norm_mix_g, norm_ffn_g, final_norm_g, mix_w_in, sgu_norm_g, sgu_w, sgu_b, mix_w_out, s5_lambda_re,
           s5_lambda_im, s5_b_re, s5_b_im, s5_c_re, s5_c_im, s5_d, s5_log_step, glu_w, glu_b, peer_wq, peer_subkeys,
           peer_u, peer_v):
    import numpy as np
    import concourse.bacc as bacc
    from concourse.bass_utils import run_bass_kernel_spmd as run

    a = np.asarray

    def states(v):
        v = a(v)
        v = v.reshape((32, 2, 64) + v.shape[2:])
        return v.transpose((1, 2, 0) + tuple(range(3, v.ndim))).reshape((P, 32) + v.shape[3:])

    log_step = np.broadcast_to(a(s5_log_step)[0][:, None], (64, 64))
    data = {
        "x": a(x).reshape(SEQ, D),
        "vecs": np.stack([a(norm_mix_g)[0], a(norm_ffn_g)[0], a(norm_mix_g)[1], a(norm_ffn_g)[1], a(final_norm_g),
                          a(s5_d)[0], a(glu_b)[0]]),
        "cst": constants(),
        "w_in": a(mix_w_in)[0],
        "sgu_g": a(sgu_norm_g)[0].reshape(1, AW),
        "sgu_wT": a(sgu_w)[0].transpose(2, 0, 1).reshape(P, 8 * P),
        "sgu_bT": a(sgu_b)[0].T,
        "w_out": a(mix_w_out)[0],
        "s5_par": np.concatenate([states(a(s5_lambda_re)[0]), states(a(s5_lambda_im)[0]), states(log_step)], axis=1),
        "s5_b": np.stack([states(a(s5_b_re)[0]).reshape(P, 512), states(a(s5_b_im)[0]).reshape(P, 512)], axis=1),
        "s5_c": np.stack([states(a(s5_c_re)[0].transpose(0, 2, 1)), states(a(s5_c_im)[0].transpose(0, 2, 1))], axis=1),
        "glu_w": a(glu_w)[0],
        "wq": a(peer_wq),
        "skT": a(peer_subkeys).transpose(3, 0, 1, 2),
        "u_tab": a(peer_u).reshape(2 * EXPERTS, D),
        "v_tab": a(peer_v).reshape(2 * EXPERTS, D),
    }
    nc = bacc.Bacc("TRN2", target_bir_lowering=False, num_devices=1)
    arrays, args = {}, []
    for name, v in data.items():
        v = np.ascontiguousarray(v)
        arrays[f"in_{name}_dram"] = v
        args.append(nc.dram_tensor(f"in_{name}_dram", v.shape, mybir.dt.from_np(v.dtype), kind="ExternalInput").ap())
    args.append(nc.dram_tensor("out_0_dram", (SEQ, D), F32, kind="ExternalOutput").ap())
    trunk(nc, *args)
    r = run(nc, [arrays], core_ids=[0])
    return r.results[0]["out_0_dram"].reshape(1, SEQ, D)
```
